# Optimizing a Trainium2 kernel written in Bass

```python
import math
import jax, jax.numpy as jnp
from jax import lax
import numpy as np
import jax
import jax.numpy as jnp

D_MODEL = 1024
BATCH = 1
SEQ = 512
DEPTH = 2

N_MIXERS = 2
N_A = (DEPTH + 1) // 2
N_B = DEPTH // 2

SSM_EXPAND = 2
D_INNER = SSM_EXPAND * D_MODEL
SSM_HEAD_DIM = 64
SSM_HEADS = D_INNER // SSM_HEAD_DIM
SSM_GROUPS = 8
SSM_HPG = SSM_HEADS // SSM_GROUPS
SSM_STATE = 128
CONV_K = 4
CONV_DIM = D_INNER + 2 * SSM_GROUPS * SSM_STATE
SSM_IN_DIM = D_INNER + CONV_DIM + SSM_HEADS
NORM_GROUP = D_INNER // SSM_GROUPS
CHUNK = 128
DT_MIN = 0.001
DT_MAX = 0.1

MLA_HEADS = 16
Q_LORA = 384
KV_LORA = 256
QK_NOPE = 64
QK_ROPE = 32
V_DIM = 64
QK_DIM = QK_NOPE + QK_ROPE
MLA_IN_DIM = Q_LORA + KV_LORA + QK_ROPE
ROPE_THETA = 10000.0
Q_BLOCK = 128

D_FF = 2816
EPS = 1e-6


def rms_norm(x, w):
    xf = x.astype(jnp.float32)
    y = xf * lax.rsqrt(jnp.mean(xf * xf, axis=-1, keepdims=True) + EPS)
    return (y * w.astype(jnp.float32)).astype(x.dtype)

def swiglu(h, w_gate, w_up, w_down):
    return (jax.nn.silu(h @ w_gate) * (h @ w_up)) @ w_down

def causal_depthwise_conv(u, w, b):
    y = lax.conv_general_dilated(u, w[:, None, :].astype(u.dtype), window_strides=(1,),
                                 padding=[(CONV_K - 1, 0)],
                                 dimension_numbers=("NWC", "WIO", "NWC"),
                                 feature_group_count=u.shape[-1])
    return y + b

def ssd_chunked(xs, dt, a, bm, cm):
    b, s = xs.shape[:2]
    nc = s // CHUNK

    def to_chunks(t):
        return jnp.swapaxes(t.reshape((b, nc, CHUNK) + t.shape[2:]), 0, 1)

    mask = jnp.tril(jnp.ones((CHUNK, CHUNK), dtype=bool))[None, :, :, None, None]

    def step(state, inp):
        xc, dtc, bc, cc = inp
        acs = jnp.cumsum(dtc * a, axis=1)
        seg = acs[:, :, None] - acs[:, None, :]
        decay = jnp.exp(jnp.where(mask, seg, -jnp.inf))
        cb = jnp.einsum("blgn,bsgn->blsg", cc, bc)
        xdt = xc * dtc[..., None]
        y_diag = jnp.einsum("blsg,blsgr,bsgrp->blgrp", cb, decay, xdt)
        y_off = jnp.einsum("blgn,bgrpn->blgrp", cc, state) * jnp.exp(acs)[..., None]
        decay_to_end = jnp.exp(acs[:, -1:] - acs)
        new_state = (state * jnp.exp(acs[:, -1])[..., None, None]
                     + jnp.einsum("bsgn,bsgr,bsgrp->bgrpn", bc, decay_to_end, xdt))
        return new_state, y_diag + y_off

    state0 = jnp.zeros((b, SSM_GROUPS, SSM_HPG, SSM_HEAD_DIM, SSM_STATE), jnp.float32)
    _, ys = lax.scan(step, state0, (to_chunks(xs), to_chunks(dt), to_chunks(bm), to_chunks(cm)))
    return jnp.swapaxes(ys, 0, 1).reshape(xs.shape)

def mamba2_mixer(h, w_in, conv_w, conv_b, dt_bias, a_log, d_skip, norm_w, w_out):
    b, s, _ = h.shape
    proj = h @ w_in
    z = proj[..., :D_INNER]
    xbc = proj[..., D_INNER:D_INNER + CONV_DIM]
    dt = proj[..., D_INNER + CONV_DIM:]
    xbc = jax.nn.silu(causal_depthwise_conv(xbc, conv_w, conv_b))
    xs = xbc[..., :D_INNER].astype(jnp.float32).reshape(b, s, SSM_GROUPS, SSM_HPG, SSM_HEAD_DIM)
    bm = xbc[..., D_INNER:D_INNER + SSM_GROUPS * SSM_STATE].astype(jnp.float32).reshape(b, s, SSM_GROUPS, SSM_STATE)
    cm = xbc[..., D_INNER + SSM_GROUPS * SSM_STATE:].astype(jnp.float32).reshape(b, s, SSM_GROUPS, SSM_STATE)
    dt = jax.nn.softplus(dt.astype(jnp.float32) + dt_bias.astype(jnp.float32)).reshape(b, s, SSM_GROUPS, SSM_HPG)
    a = (-jnp.exp(a_log.astype(jnp.float32))).reshape(SSM_GROUPS, SSM_HPG)
    y = ssd_chunked(xs, dt, a, bm, cm)
    y = y + d_skip.astype(jnp.float32).reshape(SSM_GROUPS, SSM_HPG)[:, :, None] * xs
    g = (y.reshape(b, s, D_INNER) * jax.nn.silu(z.astype(jnp.float32))).reshape(b, s, SSM_GROUPS, NORM_GROUP)
    g = g * lax.rsqrt(jnp.mean(g * g, axis=-1, keepdims=True) + EPS)
    g = g.reshape(b, s, D_INNER) * norm_w.astype(jnp.float32)
    return g.astype(h.dtype) @ w_out

def rope_cos_sin(positions):
    inv_freq = 1.0 / (ROPE_THETA ** (jnp.arange(0, QK_ROPE, 2, dtype=jnp.float32) / QK_ROPE))
    ang = positions.astype(jnp.float32)[..., None] * inv_freq
    return jnp.cos(ang), jnp.sin(ang)

def apply_rope(x, cos, sin):
    xf = x.astype(jnp.float32)
    x1, x2 = xf[..., :QK_ROPE // 2], xf[..., QK_ROPE // 2:]
    return jnp.concatenate([x1 * cos - x2 * sin, x2 * cos + x1 * sin], axis=-1).astype(x.dtype)

def causal_block_attention(q_nope, q_rope, k_nope, k_rope, v):
    s = q_nope.shape[1]
    scale = QK_DIM ** -0.5
    outs = []
    for i in range(s // Q_BLOCK):
        q0 = i * Q_BLOCK
        kend = q0 + Q_BLOCK
        sc = (jnp.einsum("bqhd,bkhd->bhqk", q_nope[:, q0:kend], k_nope[:, :kend])
              + jnp.einsum("bqhr,bkr->bhqk", q_rope[:, q0:kend], k_rope[:, :kend]))
        sc = sc.astype(jnp.float32) * scale
        qi = q0 + jnp.arange(Q_BLOCK)
        ki = jnp.arange(kend)
        sc = jnp.where(ki[None, :] <= qi[:, None], sc, -jnp.inf)
        p = jax.nn.softmax(sc, axis=-1).astype(v.dtype)
        outs.append(jnp.einsum("bhqk,bkhd->bqhd", p, v[:, :kend]))
    return jnp.concatenate(outs, axis=1)

def mla_mixer(h, positions, w_in, q_a_norm, kv_a_norm, w_q_b, w_kv_b, q_norm, k_norm, w_out):
    b, s, _ = h.shape
    proj = h @ w_in
    cq = rms_norm(proj[..., :Q_LORA], q_a_norm)
    ckv = rms_norm(proj[..., Q_LORA:Q_LORA + KV_LORA], kv_a_norm)
    k_rope = proj[..., Q_LORA + KV_LORA:]
    q = (cq @ w_q_b).reshape(b, s, MLA_HEADS, QK_DIM)
    kv = (ckv @ w_kv_b).reshape(b, s, MLA_HEADS, QK_NOPE + V_DIM)
    q_nope, q_rope = q[..., :QK_NOPE], q[..., QK_NOPE:]
    k_nope, v = kv[..., :QK_NOPE], kv[..., QK_NOPE:]
    q_nope = rms_norm(q_nope, q_norm[:QK_NOPE])
    q_rope = rms_norm(q_rope, q_norm[QK_NOPE:])
    k_nope = rms_norm(k_nope, k_norm[:QK_NOPE])
    k_rope = rms_norm(k_rope, k_norm[QK_NOPE:])
    cos, sin = rope_cos_sin(positions)
    q_rope = apply_rope(q_rope, cos[:, :, None], sin[:, :, None])
    k_rope = apply_rope(k_rope, cos, sin)
    o = causal_block_attention(q_nope, q_rope, k_nope, k_rope, v)
    return o.reshape(b, s, MLA_HEADS * V_DIM) @ w_out

def first_inputs(seed: int = 0) -> dict:
    key = jax.random.key(seed)
    ks = jax.random.split(key, 24)
    f32 = jnp.float32

    def nrm(k, shape, fan_in):
        return jax.random.normal(k, shape, f32) * fan_in ** -0.5

    def gain(k, shape):
        return 1.0 + 0.05 * jax.random.normal(k, shape, f32)

    x = jax.random.normal(ks[0], (BATCH, SEQ, D_MODEL), f32)
    offs = jax.random.randint(ks[1], (BATCH, 1), 0, 512, dtype=jnp.int32)
    positions = (jnp.arange(SEQ, dtype=jnp.int32)[None, :] + offs).astype(jnp.int32)

    norm_w = gain(ks[2], (DEPTH, 3, D_MODEL))
    ffn_w_gate = nrm(ks[3], (DEPTH, 2, D_MODEL, D_FF), D_MODEL)
    ffn_w_up = nrm(ks[4], (DEPTH, 2, D_MODEL, D_FF), D_MODEL)
    ffn_w_down = nrm(ks[5], (DEPTH, 2, D_FF, D_MODEL), D_FF)

    ssm_w_in = nrm(ks[6], (N_A, D_MODEL, SSM_IN_DIM), D_MODEL)
    ssm_conv_w = nrm(ks[7], (N_A, CONV_K, CONV_DIM), CONV_K)
    ssm_conv_b = 0.02 * jax.random.normal(ks[8], (N_A, CONV_DIM), f32)
    u = jax.random.uniform(ks[9], (N_A, SSM_HEADS), f32)
    dt0 = jnp.exp(u * (math.log(DT_MAX) - math.log(DT_MIN)) + math.log(DT_MIN))
    ssm_dt_bias = dt0 + jnp.log(-jnp.expm1(-dt0))
    ssm_a_log = jnp.log(jax.random.uniform(ks[10], (N_A, SSM_HEADS), f32, minval=1.0, maxval=16.0))
    ssm_d = 1.0 + 0.1 * jax.random.normal(ks[11], (N_A, SSM_HEADS), f32)
    ssm_norm_w = gain(ks[12], (N_A, D_INNER))
    ssm_w_out = nrm(ks[13], (N_A, D_INNER, D_MODEL), D_INNER)

    mla_w_in = nrm(ks[14], (N_B, D_MODEL, MLA_IN_DIM), D_MODEL)
    mla_q_a_norm = gain(ks[15], (N_B, Q_LORA))
    mla_kv_a_norm = gain(ks[16], (N_B, KV_LORA))
    mla_w_q_b = nrm(ks[17], (N_B, Q_LORA, MLA_HEADS * QK_DIM), Q_LORA)
    mla_w_kv_b = nrm(ks[18], (N_B, KV_LORA, MLA_HEADS * (QK_NOPE + V_DIM)), KV_LORA)
    mla_q_norm = gain(ks[19], (N_B, QK_DIM))
    mla_k_norm = gain(ks[20], (N_B, QK_DIM))
    mla_w_out = nrm(ks[21], (N_B, MLA_HEADS * V_DIM, D_MODEL), MLA_HEADS * V_DIM)

    return {"x": x, "positions": positions, "norm_w": norm_w,
            "ffn_w_gate": ffn_w_gate, "ffn_w_up": ffn_w_up, "ffn_w_down": ffn_w_down,
            "ssm_w_in": ssm_w_in, "ssm_conv_w": ssm_conv_w, "ssm_conv_b": ssm_conv_b,
            "ssm_dt_bias": ssm_dt_bias, "ssm_a_log": ssm_a_log, "ssm_d": ssm_d,
            "ssm_norm_w": ssm_norm_w, "ssm_w_out": ssm_w_out,
            "mla_w_in": mla_w_in, "mla_q_a_norm": mla_q_a_norm, "mla_kv_a_norm": mla_kv_a_norm,
            "mla_w_q_b": mla_w_q_b, "mla_w_kv_b": mla_w_kv_b, "mla_q_norm": mla_q_norm,
            "mla_k_norm": mla_k_norm, "mla_w_out": mla_w_out}

def first_block(x, positions, norm_w, ffn_w_gate, ffn_w_up, ffn_w_down,
              ssm_w_in, ssm_conv_w, ssm_conv_b, ssm_dt_bias, ssm_a_log, ssm_d,
              ssm_norm_w, ssm_w_out,
              mla_w_in, mla_q_a_norm, mla_kv_a_norm, mla_w_q_b, mla_w_kv_b,
              mla_q_norm, mla_k_norm, mla_w_out):
    for i in range(DEPTH):
        x = x + 0.5 * swiglu(rms_norm(x, norm_w[i, 0]), ffn_w_gate[i, 0], ffn_w_up[i, 0], ffn_w_down[i, 0])
        h = rms_norm(x, norm_w[i, 1])
        j = i // N_MIXERS
        if i % N_MIXERS == 0:
            x = x + mamba2_mixer(h, ssm_w_in[j], ssm_conv_w[j], ssm_conv_b[j], ssm_dt_bias[j],
                                 ssm_a_log[j], ssm_d[j], ssm_norm_w[j], ssm_w_out[j])
        else:
            x = x + mla_mixer(h, positions, mla_w_in[j], mla_q_a_norm[j], mla_kv_a_norm[j],
                              mla_w_q_b[j], mla_w_kv_b[j], mla_q_norm[j], mla_k_norm[j], mla_w_out[j])
        x = x + 0.5 * swiglu(rms_norm(x, norm_w[i, 2]), ffn_w_gate[i, 1], ffn_w_up[i, 1], ffn_w_down[i, 1])
    return x


DEPTH_2 = 1

HEAD_DIM = 64
BLOCK = 128
SWA_Q_HEADS = 8
SWA_KV_HEADS = 2
SWA_GROUP = SWA_Q_HEADS // SWA_KV_HEADS
WINDOW = 128
SWA_WIDTH = SWA_Q_HEADS * HEAD_DIM
KV_WIDTH = SWA_KV_HEADS * HEAD_DIM
LRU_WIDTH = D_MODEL // 4
LRU_BLOCKS = 8
LRU_BLOCK_W = LRU_WIDTH // LRU_BLOCKS
CONV_WIDTH = 4
LRU_C = 8.0
FOX_HEADS = 4
FOX_WIDTH = FOX_HEADS * HEAD_DIM
D_MIX = SWA_WIDTH + LRU_WIDTH + FOX_WIDTH
OFF_KA = SWA_WIDTH
OFF_VA = OFF_KA + KV_WIDTH
OFF_XB = OFF_VA + KV_WIDTH
OFF_GB = OFF_XB + LRU_WIDTH
OFF_QC = OFF_GB + LRU_WIDTH
OFF_KC = OFF_QC + FOX_WIDTH
OFF_VC = OFF_KC + FOX_WIDTH
OFF_FC = OFF_VC + FOX_WIDTH
IN_COLS = OFF_FC + FOX_HEADS
IN_SPLITS = (OFF_KA, OFF_VA, OFF_XB, OFF_GB, OFF_QC, OFF_KC, OFF_VC, OFF_FC)
N_GROUPS = 4
EXPERTS_PER_GROUP = 4
N_EXPERTS = N_GROUPS * EXPERTS_PER_GROUP
TOP_K = 2
D_EXPERT = 256
F32 = jnp.float32


def rms_normalize(x):
    xf = x.astype(F32)
    return xf * lax.rsqrt(jnp.mean(xf * xf, axis=-1, keepdims=True) + EPS)

def rms_norm_2(x, gain):
    return (rms_normalize(x) * gain.astype(F32)).astype(x.dtype)

def modulate(h, shift, scale):
    return h * (1.0 + scale[:, None, :]) + shift[:, None, :]

def alibi_slopes(n_heads):
    return jnp.exp2(-8.0 * jnp.arange(1, n_heads + 1, dtype=F32) / n_heads)

def sliding_window_sink_attention(q, k, v, sinks):
    b, s, _, dh = q.shape
    nb = s // BLOCK
    qb = q.reshape(b, nb, BLOCK, SWA_KV_HEADS, SWA_GROUP, dh)

    def band(t):
        tb = t.reshape(b, nb, BLOCK, SWA_KV_HEADS, dh)
        prev = jnp.pad(tb[:, :-1], ((0, 0), (1, 0), (0, 0), (0, 0), (0, 0)))
        return jnp.concatenate([prev, tb], axis=2)

    kb, vb = band(k), band(v)
    scores = jnp.einsum('bnqhgd,bnkhd->bnhgqk', qb, kb).astype(F32) * (dh ** -0.5)
    q_pos = BLOCK + jnp.arange(BLOCK)
    k_pos = jnp.arange(2 * BLOCK)
    dist = q_pos[:, None] - k_pos[None, :]
    in_window = (dist >= 0) & (dist < WINDOW)
    block_exists = (jnp.arange(nb)[:, None, None] > 0) | (k_pos[None, None, :] >= BLOCK)
    valid = in_window[None] & block_exists
    slopes = alibi_slopes(SWA_Q_HEADS).reshape(SWA_KV_HEADS, SWA_GROUP)
    scores = scores - slopes[:, :, None, None] * dist.astype(F32)
    scores = jnp.where(valid[None, :, None, None], scores, -jnp.inf)
    sink = jnp.broadcast_to(sinks.astype(F32).reshape(SWA_KV_HEADS, SWA_GROUP, 1, 1),
                            scores.shape[:-1] + (1,))
    probs = jax.nn.softmax(jnp.concatenate([scores, sink], axis=-1), axis=-1)[..., :-1]
    out = jnp.einsum('bnhgqk,bnkhd->bnqhgd', probs.astype(v.dtype), vb)
    return out.reshape(b, s, SWA_Q_HEADS * dh)

def causal_depthwise_conv_2(x, w, bias):
    s = x.shape[1]
    xp = jnp.pad(x, ((0, 0), (CONV_WIDTH - 1, 0), (0, 0)))
    y = bias
    for k in range(CONV_WIDTH):
        y = y + xp[:, k:k + s] * w[k]
    return y

def rg_lru(x, w_a, b_a, w_x, b_x, lam):
    b, s, w = x.shape
    xb = x.reshape(b, s, LRU_BLOCKS, LRU_BLOCK_W)
    gate_a = jnp.einsum('bsnc,ncd->bsnd', xb, w_a).reshape(b, s, w) + b_a
    gate_x = jnp.einsum('bsnc,ncd->bsnd', xb, w_x).reshape(b, s, w) + b_x
    r = jax.nn.sigmoid(gate_a.astype(F32))
    i = jax.nn.sigmoid(gate_x.astype(F32))
    log_a = -LRU_C * r * jax.nn.softplus(-lam.astype(F32))
    a = jnp.exp(log_a)
    u = jnp.sqrt(-jnp.expm1(2.0 * log_a)) * (i * x.astype(F32))

    def combine(left, right):
        a_l, u_l = left
        a_r, u_r = right
        return a_l * a_r, a_r * u_l + u_r

    _, hs = lax.associative_scan(combine, (a, u), axis=1)
    return hs.astype(x.dtype)

def forgetting_attention(q, k, v, log_f):
    b, s, h, dh = q.shape
    nb = s // BLOCK
    cum = jnp.cumsum(log_f, axis=1).transpose(0, 2, 1)
    q_blocks = q.reshape(b, nb, BLOCK, h, dh).transpose(1, 0, 2, 3, 4)
    cum_q = cum.reshape(b, h, nb, BLOCK).transpose(2, 0, 1, 3)
    k_pos = jnp.arange(s)

    def attend_block(args):
        n, q_n, cq_n = args
        logits = jnp.einsum('bqhd,bkhd->bhqk', q_n, k).astype(F32) * (dh ** -0.5)
        logits = logits + (cq_n[..., :, None] - cum[:, :, None, :])
        q_pos = n * BLOCK + jnp.arange(BLOCK)
        causal = k_pos[None, :] <= q_pos[:, None]
        logits = jnp.where(causal, logits, -jnp.inf)
        probs = jax.nn.softmax(logits, axis=-1)
        return jnp.einsum('bhqk,bkhd->bqhd', probs.astype(v.dtype), v)

    out = lax.map(attend_block, (jnp.arange(nb), q_blocks, cum_q))
    return out.transpose(1, 0, 2, 3, 4).reshape(b, s, h * dh)

def hybrid_mixer(h, w_in, w_out, out_gain, sinks, conv_w, conv_b,
                 lru_wa, lru_ba, lru_wx, lru_bx, lru_lam, fox_bf):
    b, s, _ = h.shape
    proj = jnp.einsum('bsd,de->bse', h, w_in)
    q_a, k_a, v_a, x_b, g_b, q_c, k_c, v_c, f_c = jnp.split(proj, IN_SPLITS, axis=-1)
    y_a = sliding_window_sink_attention(
        q_a.reshape(b, s, SWA_Q_HEADS, HEAD_DIM),
        k_a.reshape(b, s, SWA_KV_HEADS, HEAD_DIM),
        v_a.reshape(b, s, SWA_KV_HEADS, HEAD_DIM), sinks)
    x_conv = causal_depthwise_conv_2(x_b, conv_w, conv_b)
    y_b = rg_lru(x_conv, lru_wa, lru_ba, lru_wx, lru_bx, lru_lam) * jax.nn.gelu(g_b)
    log_f = jax.nn.log_sigmoid(f_c.astype(F32) + fox_bf.astype(F32))
    y_c = forgetting_attention(
        q_c.reshape(b, s, FOX_HEADS, HEAD_DIM),
        k_c.reshape(b, s, FOX_HEADS, HEAD_DIM),
        v_c.reshape(b, s, FOX_HEADS, HEAD_DIM), log_f)
    y = jnp.concatenate([rms_normalize(y_a), rms_normalize(y_b), rms_normalize(y_c)], axis=-1)
    y = (y * out_gain.astype(F32)).astype(h.dtype)
    return jnp.einsum('bse,ed->bsd', y, w_out)

def hierarchical_moe(h, w_rg, b_rg, w_re, b_re, w_gate, w_up, w_down):
    b, s, _ = h.shape
    group_logits = (jnp.einsum('bsd,dg->bsg', h, w_rg) + b_rg).astype(F32)
    group_prob = jax.nn.softmax(group_logits, axis=-1)
    group_p, group_idx = lax.top_k(group_prob, 1)
    expert_logits = (jnp.einsum('bsd,de->bse', h, w_re) + b_re).astype(F32)
    expert_logits = expert_logits.reshape(b, s, N_GROUPS, EXPERTS_PER_GROUP)
    in_group = jnp.take_along_axis(expert_logits, group_idx[..., None], axis=2)[:, :, 0]
    expert_prob = jax.nn.softmax(in_group, axis=-1)
    top_p, top_local = lax.top_k(expert_prob, TOP_K)
    weights = group_p * top_p / jnp.sum(top_p, axis=-1, keepdims=True)
    expert_idx = group_idx * EXPERTS_PER_GROUP + top_local
    combine = jnp.sum(jax.nn.one_hot(expert_idx, N_EXPERTS, dtype=F32) * weights[..., None], axis=-2)
    combine = combine.astype(h.dtype)
    y = jnp.zeros_like(h)
    for e in range(N_EXPERTS):
        hidden = jax.nn.silu(h @ w_gate[e]) * (h @ w_up[e])
        y = y + combine[..., e:e + 1] * (hidden @ w_down[e])
    return y

def second_inputs(seed: int = 0) -> dict:
    key = jax.random.key(seed)
    ks = jax.random.split(key, 26)
    L, D = DEPTH_2, D_MODEL

    def nrm(k, shape, scale):
        return scale * jax.random.normal(k, shape, F32)

    gate_offset = jnp.concatenate([jnp.zeros((2 * D,), F32), jnp.ones((D,), F32),
                                   jnp.zeros((2 * D,), F32), jnp.ones((D,), F32)])
    u = jax.random.uniform(ks[16], (L, LRU_WIDTH), F32, 0.9, 0.999)
    root = u ** (1.0 / LRU_C)
    lru_lam = jnp.log(root) - jnp.log1p(-root)
    return {
        'x': nrm(ks[0], (BATCH, SEQ, D), 1.0),
        'c': nrm(ks[1], (BATCH, D), 1.0),
        'w_mod': nrm(ks[2], (L, D, 6 * D), 0.25 * D ** -0.5),
        'b_mod': nrm(ks[3], (L, 6 * D), 0.1) + gate_offset,
        'norm_mix': 1.0 + nrm(ks[4], (L, D), 0.1),
        'norm_ffn': 1.0 + nrm(ks[5], (L, D), 0.1),
        'w_in': nrm(ks[6], (L, D, IN_COLS), D ** -0.5),
        'w_out': nrm(ks[7], (L, D_MIX, D), D_MIX ** -0.5),
        'out_gain': 1.0 + nrm(ks[8], (L, D_MIX), 0.1),
        'sinks': nrm(ks[9], (L, SWA_Q_HEADS), 0.5),
        'conv_w': nrm(ks[10], (L, CONV_WIDTH, LRU_WIDTH), CONV_WIDTH ** -0.5),
        'conv_b': nrm(ks[11], (L, LRU_WIDTH), 0.02),
        'lru_wa': nrm(ks[12], (L, LRU_BLOCKS, LRU_BLOCK_W, LRU_BLOCK_W), LRU_BLOCK_W ** -0.5),
        'lru_ba': nrm(ks[13], (L, LRU_WIDTH), 0.02),
        'lru_wx': nrm(ks[14], (L, LRU_BLOCKS, LRU_BLOCK_W, LRU_BLOCK_W), LRU_BLOCK_W ** -0.5),
        'lru_bx': nrm(ks[15], (L, LRU_WIDTH), 0.02),
        'lru_lam': lru_lam,
        'fox_bf': jax.random.uniform(ks[17], (L, FOX_HEADS), F32, 1.0, 5.0),
        'w_router_group': nrm(ks[18], (L, D, N_GROUPS), D ** -0.5),
        'b_router_group': nrm(ks[19], (L, N_GROUPS), 0.01),
        'w_router_expert': nrm(ks[20], (L, D, N_EXPERTS), D ** -0.5),
        'b_router_expert': nrm(ks[21], (L, N_EXPERTS), 0.01),
        'w_gate': nrm(ks[22], (L, N_EXPERTS, D, D_EXPERT), D ** -0.5),
        'w_up': nrm(ks[23], (L, N_EXPERTS, D, D_EXPERT), D ** -0.5),
        'w_down': nrm(ks[24], (L, N_EXPERTS, D_EXPERT, D), D_EXPERT ** -0.5),
        'norm_final': 1.0 + nrm(ks[25], (D,), 0.1),
    }

def second_block(x, c, w_mod, b_mod, norm_mix, norm_ffn, w_in, w_out, out_gain, sinks,
              conv_w, conv_b, lru_wa, lru_ba, lru_wx, lru_bx, lru_lam, fox_bf,
              w_router_group, b_router_group, w_router_expert, b_router_expert,
              w_gate, w_up, w_down, norm_final):
    c_act = jax.nn.silu(c)
    for l in range(DEPTH_2):
        mod = c_act @ w_mod[l] + b_mod[l]
        shift_m, scale_m, gate_m, shift_f, scale_f, gate_f = jnp.split(mod, 6, axis=-1)
        h = modulate(rms_norm_2(x, norm_mix[l]), shift_m, scale_m)
        x = x + gate_m[:, None, :] * hybrid_mixer(
            h, w_in[l], w_out[l], out_gain[l], sinks[l], conv_w[l], conv_b[l],
            lru_wa[l], lru_ba[l], lru_wx[l], lru_bx[l], lru_lam[l], fox_bf[l])
        h = modulate(rms_norm_2(x, norm_ffn[l]), shift_f, scale_f)
        x = x + gate_f[:, None, :] * hierarchical_moe(
            h, w_router_group[l], b_router_group[l], w_router_expert[l], b_router_expert[l],
            w_gate[l], w_up[l], w_down[l])
    return rms_norm_2(x, norm_final)


def setup_inputs(seed=0):
    out = dict(first_inputs(seed))
    for name, value in second_inputs(seed + 1).items():
        if name != "x":
            out[name + "_2"] = value
    return out


def reference(
    x, positions, norm_w, ffn_w_gate, ffn_w_up, ffn_w_down, ssm_w_in, ssm_conv_w, ssm_conv_b,
    ssm_dt_bias, ssm_a_log, ssm_d, ssm_norm_w, ssm_w_out, mla_w_in, mla_q_a_norm, mla_kv_a_norm,
    mla_w_q_b, mla_w_kv_b, mla_q_norm, mla_k_norm, mla_w_out, c_2, w_mod_2, b_mod_2, norm_mix_2,
    norm_ffn_2, w_in_2, w_out_2, out_gain_2, sinks_2, conv_w_2, conv_b_2, lru_wa_2, lru_ba_2,
    lru_wx_2, lru_bx_2, lru_lam_2, fox_bf_2, w_router_group_2, b_router_group_2,
    w_router_expert_2, b_router_expert_2, w_gate_2, w_up_2, w_down_2, norm_final_2,
):
    x = first_block(
        x, positions, norm_w, ffn_w_gate, ffn_w_up, ffn_w_down, ssm_w_in, ssm_conv_w,
        ssm_conv_b, ssm_dt_bias, ssm_a_log, ssm_d, ssm_norm_w, ssm_w_out, mla_w_in,
        mla_q_a_norm, mla_kv_a_norm, mla_w_q_b, mla_w_kv_b, mla_q_norm, mla_k_norm, mla_w_out,
    )
    return second_block(
        x, c_2, w_mod_2, b_mod_2, norm_mix_2, norm_ffn_2, w_in_2, w_out_2, out_gain_2, sinks_2,
        conv_w_2, conv_b_2, lru_wa_2, lru_ba_2, lru_wx_2, lru_bx_2, lru_lam_2, fox_bf_2,
        w_router_group_2, b_router_group_2, w_router_expert_2, b_router_expert_2, w_gate_2,
        w_up_2, w_down_2, norm_final_2,
    )


_drawn_inputs = setup_inputs


def setup_inputs(seed=0):
    import zlib

    import numpy as np

    out = dict(_drawn_inputs(seed))
    spreads = {}
    factors = {'mla_q_a_norm': 5.921,
     'mla_kv_a_norm': 3.462,
     'mla_q_norm': 5.507,
     'mla_k_norm': 5.454,
     'lru_ba_2': 64.0,
     'lru_bx_2': 50.66,
     'b_router_group_2': 18.292,
     'b_router_expert_2': 53.933,
     'norm_ffn_2': 2.84,
     'sinks_2': 3.836,
     'conv_b_2': 5.262}
    for name, (base, spread) in spreads.items():
        noise = np.random.default_rng([zlib.crc32(name.encode()), seed]).standard_normal(out[name].shape)
        drawn = base * np.exp(spread * noise) if base else spread * noise
        out[name] = jnp.asarray(drawn.astype(out[name].dtype))
    for name, factor in factors.items():
        out[name] = (out[name] * factor).astype(out[name].dtype)
    return out
```

```python
from contextlib import ExitStack, contextmanager

import concourse.bass as bass
import concourse.mybir as mybir
from concourse.alu_op_type import AluOpType as ALU

F32 = mybir.dt.float32
F32R = mybir.dt.float32r
I32 = mybir.dt.int32
ACT = mybir.ActivationFunctionType
AX = mybir.AxisListType.X

P = 128
T = 512
NT = T // P
D = 1024
KD = D // P
EPS = 1e-6
NEG = -1e30

D_FF = 2816
HALF_FF = D_FF // P // 2

D_INNER = 2048
GROUPS, HEADS_PER_GROUP, HEAD_P, STATE = 8, 4, 64, 128
CONV_DIM = D_INNER + 2 * GROUPS * STATE
CONV_TILES = CONV_DIM // P
CONV_K = 4
SSM_HEADS = GROUPS * HEADS_PER_GROUP

MLA_HEADS, Q_LORA, KV_LORA, NOPE, ROPE, V_DIM = 16, 384, 256, 64, 32, 64
QK = NOPE + ROPE
HR = ROPE // 2

SWA_HEADS, SWA_KV, FOX_HEADS, HEAD_DIM = 8, 2, 4, 64
LRU = 256
N_GROUPS, PER_GROUP, N_EXPERTS, D_EXPERT = 4, 4, 16, 256
LRU_C = 8.0

RING_K = 11
PI = 3.141592653589793
TWO_PI_HI = 6.28125
TWO_PI_LO = 2 * PI - TWO_PI_HI


def cut(start, n):
    return slice(start, start + n) if isinstance(start, int) else bass.ds(start, n)


class Signals:

    def __init__(self, nc, per_turn):
        self.nc, self.per_turn, self.counted = nc, per_turn, {}
        self.sems, self.total, self.turn, self.loop = {}, {}, {}, None
        self.passed = nc.alloc_semaphore("passed")
        self.n_loops = 0
        self.recent = {}
        for name in sorted(n for loop, n in per_turn if loop == "start"):
            self.sems[name] = nc.alloc_semaphore(name.replace(" ", "_"))
            nc.gpsimd.sem_inc(self.sems[name], 1)
            self.total[name] = 1
            self.counted["start", name] = 1

    def done(self, name, instruction, by=1):
        if name not in self.sems:
            self.sems[name] = self.nc.alloc_semaphore(name.replace(" ", "_"))
        instruction.then_inc(self.sems[name], by)
        self.recent[str(instruction.ins.engine)] = name
        count = self.turn if self.loop else self.total
        count[name] = count.get(name, 0) + by
        return instruction

    def now(self, name):
        assert not self.loop
        return name, self.total[name]

    def need(self, engine, *names):
        waits = []
        for name in names:
            if not isinstance(name, str):
                waits.append(name)
                continue
            value = self.total.get(name, 0)
            if self.loop:
                which, i = self.loop
                value += self.turn.get(name, 0)
                per = self.per_turn.get((which, name), 0)
                if per:
                    if value == 0:
                        self.counted["start", name] = 1
                    waits.append((name, i * per + value))
                    continue
            if value:
                waits.append((name, value))
        for name, value in waits:
            if name not in self.sems:
                self.sems[name] = self.nc.alloc_semaphore(name.replace(" ", "_"))
            engine.wait_ge(self.sems[name], value)
        if engine in (self.nc.gpsimd, self.nc.sync) and any(not isinstance(value, int) for _, value in waits):
            engine.sem_inc(self.passed, 1)

    @contextmanager
    def turns(self, n):
        which = self.n_loops
        self.n_loops += 1
        with self.nc.Fori(0, n) as i:
            self.loop, self.turn = (which, i), {}
            yield i
            self.loop = None
        for name, k in self.turn.items():
            self.counted[which, name] = k
            self.total[name] = self.total.get(name, 0) + n * k


class Program:
    def __init__(self, nc, ins, out, per_turn):
        self.nc, self.d, self.out = nc, ins, out
        self.sig = Signals(nc, per_turn)
        self.done, self.need = self.sig.done, self.sig.need
        self.te, self.ve, self.ae, self.ge, self.se = nc.tensor, nc.vector, nc.scalar, nc.gpsimd, nc.sync
        self.base = (nc.sbuf_base + 63) // 64 * 64
        self.n_names = 0
        self.units = 0

    def sb(self, name, shape, dt=F32):
        size = 4
        for n in shape[1:]:
            size *= n
        self.n_names += 1
        t = self.nc.alloc_sbuf_tensor_at(f"{name}_{self.n_names}", list(shape), dt, offset=self.base)
        self.base += (size + 31) // 32 * 32
        assert self.base <= self.nc.sbuf_usable_end, (name, self.base)
        return t

    @contextmanager
    def stage(self):
        mark = self.base
        yield
        self.base = mark

    def v(self, instruction, name="dve"):
        return self.done(name, instruction)

    def a(self, instruction, name="act"):
        return self.done(name, instruction)

    def settle(self):
        names = [n for e, n in self.sig.recent.items() if "PE" in e or "DVE" in e or "Activation" in e]
        for e in (self.te, self.ve, self.ae):
            self.need(e, *names)

    def setup(self):
        nc, d = self.nc, self.d
        sb, done, need = self.sb, self.done, self.need
        te, ve, ae, ge, se = self.te, self.ve, self.ae, self.ge, self.se
        self.bank = [nc.alloc_psum_tensor(f"bank{b}", [P, T], F32) for b in range(8)]
        self.x = sb("x", [P, KD, T])
        self.h_at = self.base
        self.h_hi = sb("h_hi", [P, KD, T], F32R)
        self.h_lo = sb("h_lo", [P, KD, T], F32R)
        self.h_end = self.base
        self.raw = sb("raw", [P, 2, RING_K * P])
        self.w_hi = sb("w_hi", [P, 2, RING_K * P], F32R)
        self.w_lo = sb("w_lo", [P, 2, RING_K * P], F32R)
        self.nr = sb("norm_r", [P, T])
        self.nsq = sb("norm_sq", [P, 2, T])
        self.nacc = sb("norm_acc", [P, T])
        self.nht = sb("norm_ht", [P, 2, T])
        self.ident = sb("ident", [P, P])
        self.ones = sb("ones", [P, P])
        self.causal01 = sb("causal01", [P, P])
        self.ident_r = sb("ident_r", [P, P], F32R)
        self.ones_r = sb("ones_r", [P, P], F32R)
        self.causal_r = sb("causal_r", [P, 3 * P], F32R)
        done("const", ge.memset(self.ident[:, :], 0.0))
        done("const", ge.memset(self.ones[:, :], 1.0))
        done("const", ge.memset(self.causal01[:, :], 1.0))
        masks = self.nacc
        done("const", ge.memset(masks[:, 0:3 * P], 0.0))
        need(ge, "const")
        done("const", ge.affine_select(out=self.ident[:, :], in_=self.ident[:, :], compare_op=ALU.not_equal, fill=1.0,
                                       base=0, pattern=[[-1, P]], channel_multiplier=1))
        done("const", ge.affine_select(out=self.causal01[:, :], in_=self.causal01[:, :], compare_op=ALU.is_ge, fill=0.0,
                                       base=0, pattern=[[1, P]], channel_multiplier=-1))
        for block, sign in ((masks[:, 0:P], -1), (masks[:, 2 * P:3 * P], 1)):
            done("const", ge.affine_select(out=block, in_=block, compare_op=ALU.is_ge, fill=NEG, base=0, pattern=[[-sign, P]],
                                           channel_multiplier=sign))
        need(ve, "const")
        for rounded, exact in ((self.ident_r, self.ident[:, :]), (self.ones_r, self.ones[:, :]), (self.causal_r, masks[:, 0:3 * P])):
            self.v(ve.tensor_copy(rounded[:, :], exact), "rounded")
        rows = [("norm_w", d["norm_w"].rearrange("a b (k p) -> (a b k) p", p=P), 48),
                ("ssm_conv_b", d["ssm_conv_b"].rearrange("a (k p) -> (a k) p", p=P), 32),
                ("ssm_norm_w", d["ssm_norm_w"].rearrange("a (k p) -> (a k) p", p=P), 16),
                ("q_a", d["mla_q_a_norm"].rearrange("a (k p) -> (a k) p", p=P), 3),
                ("kv_a", d["mla_kv_a_norm"].rearrange("a (k p) -> (a k) p", p=P), 2),
                ("norm_mix", d["norm_mix_2"].rearrange("a (k p) -> (a k) p", p=P), 8),
                ("norm_ffn", d["norm_ffn_2"].rearrange("a (k p) -> (a k) p", p=P), 8),
                ("out_gain", d["out_gain_2"].rearrange("a (k p) -> (a k) p", p=P), 8),
                ("conv_w_2", d["conv_w_2"].rearrange("a c (k p) -> (a c k) p", p=P), 8),
                ("conv_b_2", d["conv_b_2"].rearrange("a (k p) -> (a k) p", p=P), 2),
                ("lru_ba", d["lru_ba_2"].rearrange("a (k p) -> (a k) p", p=P), 2),
                ("lru_bx", d["lru_bx_2"].rearrange("a (k p) -> (a k) p", p=P), 2),
                ("lru_lam", d["lru_lam_2"].rearrange("a (k p) -> (a k) p", p=P), 2),
                ("b_mod", d["b_mod_2"].rearrange("a (k p) -> (a k) p", p=P), 48),
                ("norm_final", d["norm_final_2"].rearrange("(k p) -> k p", p=P), 8),
                ("c", d["c_2"].rearrange("a (k p) -> (a k) p", p=P), 8),
                ("ssm_conv_w", d["ssm_conv_w"].rearrange("a c (k p) -> (a c k) p", p=P), 128)]
        cols = sb("cols", [P, 3, P])
        self.col_at = {}
        with self.stage():
            xn = sb("x_natural", [P, NT, D])
            for tt in range(NT):
                done("load x", se.dma_start(xn[:, tt, :], d["x"][0, tt * P:(tt + 1) * P, :]), 16)
            table = sb("table", [P, 3, P])
            done("const", ge.memset(table[:, :, :], 0.0))
            need(ae, "const")
            t, r = 0, 0
            for name, ap, n in rows:
                if r + n > P:
                    t, r = t + 1, 0
                done("load table", ae.dma_start(table[r:r + n, t, :], ap), 16)
                self.col_at[name] = (t, r)
                r += n
            need(te, "load x", "load table", "const")
            for t in range(3):
                ins = te.transpose(self.bank[0][:, t * P:(t + 1) * P], table[:, t, :], self.ident[:, :])
            done("pe", ins)
            need(ve, "pe")
            self.v(ve.tensor_copy(cols[:, :, :].rearrange("p a b -> p (a b)"), self.bank[0][:, 0:3 * P]), "cols")
            for k in range(KD):
                b = 1 + k % 7
                if k == 7:
                    need(te, "x tile")
                for tt in range(NT):
                    ins = te.transpose(self.bank[b][:, tt * P:(tt + 1) * P], xn[:, tt, k * P:(k + 1) * P], self.ident[:, :])
                done("pe", ins)
                need(ve, "pe")
                self.v(ve.tensor_copy(self.x[:, k, :], self.bank[b][:, :]), "x tile")
                if k == 0:
                    need(ae, "rounded")
                self.add_square(self.x[:, k, :], k % 2, "x tile", first=k == 0)
            self.settle()
        self.cols = cols

    def col(self, name, k, n=1):
        t, r = self.col_at[name]
        return self.cols[:, t, cut(r + k, n)]

    def mask_keys(self, j, n):
        c = max(0, n - 2) * P
        return [(self.ident_r[:, :], self.causal_r[:, (3 - min(n, 2)) * P:], c)]

    def mask_queries(self, n):
        return [(self.ident_r[:, :], self.causal_r[:, 0:min(n, 2) * P], 0)]

    def unit(self, sources, kt, banks, rhs, start=True, stop=True, ready=None):
        s = self.units % 2
        self.units += 1
        mt = len(banks)
        view = lambda t: t[:, s, 0:kt * mt * P].rearrange("p (k m) -> p k m", k=kt)
        raw, hi, lo = view(self.raw), view(self.w_hi), view(self.w_lo)
        flat = lambda t: t[:, s, 0:kt * mt * P]
        self.need(self.se, f"split {s}")
        for ap, c in sources:
            ins = self.se.dma_start(raw[:, :, c:c + ap.shape[-1]], ap.rearrange("(k p) m -> p k m", p=P))
            self.done(f"load {s}", ins, 16)
        self.need(self.ge, f"load {s}", f"unit {s}")
        self.done("pool", self.ge.tensor_scalar(flat(self.w_hi), flat(self.raw), 1.0, 0.0, ALU.mult, ALU.add))
        self.need(self.ge, "pool")
        self.done(f"split {s}", self.ge.tensor_tensor(flat(self.w_lo), flat(self.raw), flat(self.w_hi).bitcast(F32), ALU.subtract))
        self.need(self.te, f"split {s}", *([f"bank {b}" for b in banks] if start else []))
        for m, b in enumerate(banks):
            for k in range(kt):
                if ready and m == 0:
                    self.need(self.te, *ready[k])
                x_hi, x_lo = rhs(k)
                first, last = start and k == 0, stop and k == kt - 1
                cols = slice(m * P, (m + 1) * P)
                self.te.matmul(self.bank[b][:, :], hi[:, k, cols], x_hi, start=first, stop=False)
                self.te.matmul(self.bank[b][:, :], hi[:, k, cols], x_lo, start=False, stop=False)
                ins = self.te.matmul(self.bank[b][:, :], lo[:, k, cols], x_hi, start=False, stop=last)
        self.done(f"unit {s}", ins)
        return f"unit {s}"

    def h(self, k):
        return self.h_hi[:, k, :], self.h_lo[:, k, :]

    def split_tile(self, src, hi, lo, ready, name="split tile"):
        self.need(self.ae, ready)
        self.a(self.ae.activation(hi, src, ACT.Copy), name + " hi")
        self.need(self.ve, ready, name + " hi")
        self.v(self.ve.tensor_tensor(lo, src, hi.bitcast(F32), ALU.subtract), name + " lo")

    def add_square(self, tile, s, ready, first=False):
        need = self.need
        need(self.ae, ready, f"square used {s}", *(["ones read"] if first else []))
        self.a(self.ae.activation(self.nacc[:, :] if first else self.nsq[:, s, :], tile, ACT.Square), "square")
        need(self.ve, "square")
        if not first:
            need(self.ve, f"square used {1 - s}")
            self.v(self.ve.tensor_tensor(self.nacc[:, :], self.nacc[:, :], self.nsq[:, s, :], ALU.add), f"square used {s}")

    def clear_squares(self):
        self.need(self.ve, "ones read")
        self.v(self.ve.memset(self.nacc[:, :], 0.0), "square used 0")

    def inverse_rms(self, tiles, n, bank, ready):
        te, ae, need = self.te, self.ae, self.need
        ae.preload_act_table_set("natural_log_exp_and_others")
        for k, tile in enumerate(tiles):
            self.add_square(tile, k % 2, ready, first=k == 0)
        need(te, "square", "square used 0", "square used 1", f"bank {bank}")
        self.done("ones read", te.matmul(self.bank[bank][:, :], self.ones[:, :], self.nacc[:, :], start=True, stop=True))
        need(ae, "ones read", "scaled")
        self.a(ae.activation(self.nr[:, :], self.bank[bank][:, :], ACT.Ln, bias=self.eps[:, 0:1], scale=1.0 / n), f"bank {bank}")
        need(ae, f"bank {bank}")
        self.a(ae.activation(self.nr[:, :], self.nr[:, :], ACT.Exp, scale=-0.5), "inverse rms")

    def norm_to_h(self, gain, shift=None):
        te, ve, ae, ge, need = self.te, self.ve, self.ae, self.ge, self.need
        self.inverse_rms([], D, 7, None)
        ready = []
        for k in range(KD):
            t, hi, lo = self.nht[:, k % 2, :], self.h_hi[:, k, :], self.h_lo[:, k, :]
            on = ge if k % 2 and shift is None else ve
            need(ve, "inverse rms", f"h hi {k % 2}", f"h lo {k % 2}")
            self.v(ve.scalar_tensor_tensor(t, self.x[:, k, :], gain(k), self.nr[:, :], ALU.mult, ALU.mult), "scaled")
            need(ae, "scaled")
            if shift is None:
                self.a(ae.activation(hi, t, ACT.Copy), f"h hi {k % 2}")
                need(on, "scaled", f"h hi {k % 2}")
                self.done(f"h lo {k % 2}", on.tensor_tensor(lo, t, hi.bitcast(F32), ALU.subtract))
            else:
                self.a(ae.activation(hi, t, ACT.Identity, bias=shift(k)), f"h hi {k % 2}")
                need(ve, "scaled", f"h hi {k % 2}")
                self.v(ve.scalar_tensor_tensor(lo, t, shift(k), hi.bitcast(F32), ALU.add, ALU.subtract), f"h lo {k % 2}")
            ready.append((self.sig.now(f"h hi {k % 2}"), self.sig.now(f"h lo {k % 2}")))
        need(ve, "scaled", "h lo 0", "h lo 1")
        need(ae, "scaled", "h lo 0", "h lo 1")
        return ready

    def residual(self, m, e, unit, gate, squares):
        self.need(self.ve, unit)
        tile = self.x[:, cut(m, 1), :]
        self.v(self.ve.scalar_tensor_tensor(tile, self.bank[e][:, :].unsqueeze(1), gate, tile, ALU.mult, ALU.add), f"bank {e}")
        if squares:
            self.need(self.ae, f"bank {e}", f"square used {e % 2}")
            self.a(self.ae.activation(self.nsq[:, e % 2, :].unsqueeze(1), tile, ACT.Square), "square")
            self.need(self.ve, "square", f"square used {1 - e % 2}")
            self.v(self.ve.tensor_tensor(self.nacc[:, :], self.nacc[:, :], self.nsq[:, e % 2, :], ALU.add), f"square used {e % 2}")

    def small_setup(self):
        ve, ae, need = self.ve, self.ae, self.need
        self.eps = self.sb("eps", [P, 1])
        self.mod = self.sb("mod", [P, 48])
        self.c_act = self.sb("c_act", [P, KD])
        self.v(ve.memset(self.eps[:, :], EPS), "cols")
        need(ve, "cols", "const")
        need(ae, "cols", "const")
        need(self.te, "const")
        self.a(ae.activation(self.c_act[:, :], self.col("c", 0, KD), ACT.Silu), "c act")
        need(ve, "c act")

    def ffn(self, l, i, mod_tiles=None):
        d, need, te, ve, ae = self.d, self.need, self.te, self.ve, self.ae
        ready = self.norm_to_h(lambda k: self.col("norm_w", (l * 3 + 2 * i) * KD + k))
        wg, wu, wd = d["ffn_w_gate"][l, i], d["ffn_w_up"][l, i], d["ffn_w_down"][l, i]
        with self.stage():
            g_hi = self.sb("g_hi", [P, HALF_FF, T], F32R)
            g_lo = self.sb("g_lo", [P, HALF_FF, T], F32R)
            act = self.sb("act", [P, T])
            prod = self.sb("prod", [P, T])

            def pair(half, j, ready=None):
                c = j * P + half * HALF_FF * P
                if mod_tiles is not None:
                    self.mod_load(mod_tiles[half], j)
                gate = self.unit([(wg[:, cut(c, P)], 0)], KD, [0], self.h, ready=ready)
                need(ae, gate, "prod")
                self.a(ae.activation(act[:, :], self.bank[0][:, :], ACT.Silu), "bank 0")
                up = self.unit([(wu[:, cut(c, P)], 0)], KD, [1], self.h)
                need(ve, up, "bank 0", "g hi", "g lo")
                self.v(ve.tensor_tensor(prod[:, :], act[:, :], self.bank[1][:, :], ALU.mult), "bank 1")
                need(ae, "bank 1")
                self.a(ae.activation(g_hi[:, cut(j, 1), :], prod[:, :].unsqueeze(1), ACT.Copy), "g hi")
                need(ve, "bank 1", "g hi")
                self.v(ve.tensor_tensor(g_lo[:, cut(j, 1), :], prod[:, :].unsqueeze(1), g_hi[:, cut(j, 1), :].bitcast(F32), ALU.subtract), "prod")
                if mod_tiles is not None:
                    self.mod_add(mod_tiles[half], j)

            for half in range(2):
                if half == 0:
                    pair(0, 0, ready)
                    with self.sig.turns(HALF_FF - 1) as j:
                        pair(0, j + 1)
                else:
                    with self.sig.turns(HALF_FF) as j:
                        pair(1, j)
                if mod_tiles is not None:
                    self.mod_load(mod_tiles[half], HALF_FF)
                    self.mod_add(mod_tiles[half], HALF_FF)
                if half:
                    self.clear_squares()
                need(te, "prod", "g hi")
                with self.sig.turns(KD // 2) as m2:
                    for e in range(2):
                        m = m2 * 2 + e
                        unit = self.unit([(wd[half * HALF_FF * P:(half + 1) * HALF_FF * P, cut(m * P, P)], 0)], HALF_FF, [2 + e],
                                         lambda k: (g_hi[:, k, :], g_lo[:, k, :]))
                        self.residual(m, 2 + e, unit, 0.5, squares=half == 1)

    def mod_load(self, tiles, j):
        ae, need = self.ae, self.need
        need(ae, "mod added")
        w = self.d["w_mod_2"][0, tiles[0] * P:(tiles[1] + 1) * P, cut(j * 512, 512)].rearrange("(k p) m -> p k m", p=P)
        self.done("load mod", ae.dma_start(self.mod_w[:, :, :], w), 16)

    def mod_add(self, tiles, j):
        ve, need = self.ve, self.need
        for e in range(2):
            need(ve, "load mod", "mod added", "mod set")
            acc = self.mod_acc[:, cut(j * 512, 512)]
            self.v(ve.scalar_tensor_tensor(acc, self.mod_w[:, e, :], self.c_act[:, tiles[e]:tiles[e] + 1], acc, ALU.mult, ALU.add), "mod added")

    def mod_begin(self):
        self.mod_base = self.base
        self.mod_acc = self.sb("mod_acc", [P, 6 * D])
        self.mod_w = self.sb("mod_w", [P, 2, 512])
        self.v(self.ve.memset(self.mod_acc[:, :], 0.0), "mod set")

    def mod_end(self):
        te, ve, need = self.te, self.ve, self.need
        need(te, "mod added", "bank 6")
        for n in range(48):
            ins = te.matmul(self.bank[6][:, n:n + 1], self.mod_acc[:, n * P:(n + 1) * P], self.ones[:, 0:1], start=True, stop=True)
        self.done("pe", ins)
        need(ve, "pe")
        self.v(ve.tensor_tensor(self.mod[:, 0:48], self.bank[6][:, 0:48], self.col("b_mod", 0, 48), ALU.add), "bank 6")
        need(ve, "bank 6")
        for n, name in ((8, "norm_mix"), (32, "norm_ffn")):
            self.v(ve.scalar_tensor_tensor(self.mod[:, n:n + 8], self.mod[:, n:n + 8], 1.0, self.col(name, 0, 8), ALU.add, ALU.mult), "mod gains")
        need(ve, "mod gains")
        need(self.ae, "mod gains", "bank 6")
        need(self.ge, "mod gains")
        self.base = self.mod_base


def finish(pr):
    te, ve, ae, se, need = pr.te, pr.ve, pr.ae, pr.se, pr.need
    with pr.stage():
        r, yt = pr.nr, pr.nht
        yn = pr.sb("yn", [P, NT, D])
        pr.inverse_rms([], D, 7, None)
        for k in range(KD):
            need(ve, "inverse rms", f"turned {k % 2}", "h lo 0", "h lo 1")
            pr.v(ve.scalar_tensor_tensor(yt[:, k % 2, :], pr.x[:, k, :], pr.col("norm_final", k), r[:, :], ALU.mult, ALU.mult), "final")
            need(te, "final", f"bank {k % 2}")
            for tt in range(NT):
                ins = te.transpose(pr.bank[k % 2][:, tt * P:(tt + 1) * P], yt[:, k % 2, tt * P:(tt + 1) * P], pr.ident[:, :])
            pr.done(f"turned {k % 2}", ins)
            need(ae, f"turned {k % 2}")
            pr.a(ae.copy(yn[:, :, k * P:(k + 1) * P], pr.bank[k % 2][:, :].rearrange("p (a b) -> p a b", a=NT)), f"bank {k % 2}")
        need(se, "bank 0", "bank 1")
        for tt in range(NT):
            pr.done("store", se.dma_start(pr.out[0, tt * P:(tt + 1) * P, :], yn[:, tt, :]), 16)
        need(se, "store")


def softplus(pr, out, z, tmp, rows, ready, name):
    ve, ae, need = pr.ve, pr.ae, pr.need
    e, u, t = tmp
    need(ae, ready)
    pr.a(ae.activation(e, z, ACT.Abs))
    need(ae, "act")
    pr.a(ae.activation(e, e, ACT.Exp, scale=-1.0))
    need(ve, "act", ready)
    pr.v(ve.tensor_scalar(u, e, 1.0, None, ALU.add))
    need(ve, "dve")
    pr.v(ve.tensor_scalar(t, u, -1.0, None, ALU.add))
    need(ve, "dve")
    need(ae, "dve")
    pr.v(ve.tensor_tensor(t, e, t, ALU.subtract))
    pr.a(ae.activation(u, u, ACT.Ln))
    need(ve, "dve", "act")
    pr.v(ve.tensor_tensor(t, t, u, ALU.add))
    need(ve, "dve")
    pr.v(ve.scalar_tensor_tensor(out, z, 0.0, t, ALU.max, ALU.add), name)


def ssm(pr):
    te, ve, ae, ge, se, need, d = pr.te, pr.ve, pr.ae, pr.ge, pr.se, pr.need, pr.d
    v, a, done, bank, sb = pr.v, pr.a, pr.done, pr.bank, pr.sb
    HG = HEADS_PER_GROUP
    w_in = d["ssm_w_in"][0]
    w_out = d["ssm_w_out"][0]
    ready = pr.norm_to_h(lambda k: pr.col("norm_w", 1 * KD + k))
    pr.settle()
    with pr.stage():
        y_hi = sb("y_hi", [P, D_INNER // P, T], F32R)
        y_lo = sb("y_lo", [P, D_INNER // P, T], F32R)
        grp = sb("grp", [P, 2, 6, T])
        u = sb("u", [P, 2, CONV_K - 1 + T])
        conv = pr.nsq
        acs_t = sb("acs_t", [SSM_HEADS, T])
        dt_n = sb("dt_n", [P, NT, SSM_HEADS])
        acs_n = sb("acs_n", [P, NT, SSM_HEADS])
        dte_n = sb("dte_n", [P, NT, SSM_HEADS])
        cd_all = sb("cd_all", [P, NT, SSM_HEADS])
        dcol = sb("dcol", [P, D_INNER // P])
        sel = sb("sel", [SSM_HEADS, HG, P])
        nat = sb("nat", [P, P])
        xdt = sb("xdt", [P, HG, HEAD_P])
        xde = sb("xde", [P, HG, HEAD_P])
        cbm = sb("cbm", [P, P])
        by_heads = lambda t: t.rearrange("p (a b) -> p a b", a=HG)
        ec = by_heads(pr.nacc[:, :])
        seg = sb("seg", [P, HG, P])
        lt = sb("lt", [P, HG, P])
        cte = sb("cte", [P, HG, P])
        state = sb("state", [P, HG, HEAD_P])
        yy = pr.nht

        v(ve.memset(u[:, :, 0:CONV_K - 1], 0.0), "u set")
        flat = lambda t: t[:, :, :].rearrange("p a b -> p (a b)")
        rows = lambda t: flat(t)[0:SSM_HEADS, :]
        dt_t, z_t, tmp = yy[0:SSM_HEADS, 0, :], rows(seg), (rows(lt), rows(cte), rows(ec))
        last, small = cbm, nat[0:SSM_HEADS, 0:2]
        done("load small", ae.dma_start(small[:, 0:1], d["ssm_dt_bias"].rearrange("a h -> h a")), 16)
        done("load small", ae.dma_start(small[:, 1:2], d["ssm_a_log"].rearrange("a h -> h a")), 16)
        for e in range(2):
            src = d["ssm_d"].rearrange("a (k e) -> (a e) k", e=2)[e]
            done("load small", ae.dma_start(dcol[e * 64:(e + 1) * 64, :], src.partition_broadcast(64), allow_slow_non_contiguous=True), 16)
        done("last set", ge.memset(last[:, :], 0.0))
        need(ge, "last set")
        done("last set", ge.affine_select(out=last[:, :], in_=last[:, :], compare_op=ALU.not_equal, fill=1.0,
                                          base=-(P - 1), pattern=[[0, P]], channel_multiplier=1))
        unit = pr.unit([(w_in[:, D_INNER + CONV_DIM:], 0), (w_in[:, 0:P - SSM_HEADS], SSM_HEADS)], KD, [0], pr.h, ready=ready)
        need(ve, unit, "load small")
        v(ve.tensor_scalar(z_t, bank[0][0:SSM_HEADS, :], small[:, 0:1], None, ALU.add), "bank 0")
        softplus(pr, dt_t, z_t, tmp, SSM_HEADS, "bank 0", "dt")
        a(ae.activation(small[:, 1:2], small[:, 1:2], ACT.Exp), "a")
        need(ve, "dt", "a")
        v(ve.tensor_scalar(z_t, dt_t, small[:, 1:2], -1.0, ALU.mult, ALU.mult))
        need(ve, "dve")
        need(ve, "const")
        for c in range(NT):
            cs = slice(c * P, (c + 1) * P)
            v(ve.tensor_tensor_scan(acs_t[:, cs], pr.ones[0:SSM_HEADS, :], z_t[:, cs], 0.0, ALU.mult, ALU.add), "acs")
        need(te, "acs", "dt", "bank 1")
        for c in range(NT):
            cs = slice(c * P, (c + 1) * P)
            te.transpose(bank[1][:, c * SSM_HEADS:(c + 1) * SSM_HEADS], dt_t[:, cs], pr.ident[0:SSM_HEADS, 0:SSM_HEADS])
            ins = te.transpose(bank[1][:, P + c * SSM_HEADS:P + (c + 1) * SSM_HEADS], acs_t[:, cs], pr.ident[0:SSM_HEADS, 0:SSM_HEADS])
        done("pe", ins)
        need(ve, "pe")
        v(ve.tensor_copy(flat(dt_n), bank[1][:, 0:P]))
        v(ve.tensor_copy(flat(acs_n), bank[1][:, P:2 * P]), "bank 1")
        need(te, "bank 1", "bank 2", "last set")
        done("pe", te.matmul(bank[2][:, 0:P], last[:, :], flat(acs_n), start=True, stop=True))
        need(ve, "pe", "bank 1")
        v(ve.tensor_tensor(flat(dte_n), bank[2][:, 0:P], flat(acs_n), ALU.subtract), "end set")
        need(ae, "end set")
        a(ae.activation(flat(cd_all), bank[2][:, 0:P], ACT.Exp), "bank 2")
        a(ae.activation(flat(dte_n), flat(dte_n), ACT.Exp), "decay")
        need(ve, "decay", "bank 2")
        v(ve.tensor_tensor(flat(dte_n), flat(dte_n), flat(dt_n), ALU.mult), "decay set")
        need(ve, "decay set", "load small")
        need(te, "decay set")
        need(ae, "decay set")

        def project(g, n, b):
            column = [D_INNER + g * 256, D_INNER + g * 256 + P, 2 * D_INNER + g * P, 2 * D_INNER + (GROUPS + g) * P,
                      g * 256, g * 256 + P][n]
            return pr.unit([(w_in[:, cut(column, P)], 0)], KD, [b], pr.h)

        def take(par, n, b, unit):
            if n >= 4:
                need(ae, unit, "gated")
                a(ae.activation(grp[:, par, n, :], bank[b][:, :], ACT.Silu), f"bank {b}")
            else:
                need(ae, unit, f"conv {b}", "u set")
                a(ae.copy(u[:, b, CONV_K - 1:], bank[b][:, :]), f"bank {b}")

        def convolve(g, par, n, b):
            tile = [2 * g, 2 * g + 1, 16 + g, 24 + g][n]
            tap = lambda k: pr.col("ssm_conv_w", CONV_TILES * k + tile)
            need(ve, f"bank {b}", f"silu {b}")
            v(ve.tensor_scalar(conv[:, b, :], u[:, b, CONV_K - 1:], tap(3), pr.col("ssm_conv_b", tile), ALU.mult, ALU.add))
            for k in range(CONV_K - 1):
                need(ve, "dve")
                v(ve.scalar_tensor_tensor(conv[:, b, :], u[:, b, k:k + T], tap(k), conv[:, b, :], ALU.mult, ALU.add),
                  f"conv {b}" if k == CONV_K - 2 else "dve")
            need(ae, f"conv {b}", "X", "CB", "CTE", "gated")
            a(ae.activation(grp[:, par, n, :], conv[:, b, :], ACT.Silu), f"silu {b}")

        def chunk_products(g, par, c):
            cs = slice(c * P, (c + 1) * P)
            if c == 0:
                need(ve, "ACS", "const")
                v(ve.tensor_copy(sel[:, :, :], pr.ident[0:SSM_HEADS, cut(g * HG, HG)].unsqueeze(2).broadcast_to([SSM_HEADS, HG, P])), "sel")
            need(te, "bank 4", "sel")
            for h in range(HG):
                ins = te.matmul(bank[4][:, h * P:(h + 1) * P], sel[:, h, :], acs_t[:, cs], start=True, stop=True)
            done("ACS", ins)
            need(te, "bank 2", "silu 0", "silu 1")
            for n in range(3):
                ins = te.transpose(bank[2][:, n * P:(n + 1) * P], grp[:, par, n, cs], pr.ident[:, :])
            done("X", ins)
            need(te, "bank 3")
            done("CB", te.matmul(bank[3][:, 0:P], grp[:, par, 2, cs], grp[:, par, 3, cs], start=True, stop=True))

        def chunk_decays(g, par, c):
            cs = slice(c * P, (c + 1) * P)
            heads = cut(g * HG, HG)
            bank4 = by_heads(bank[4][:, :])
            need(ve, "ACS", "LT")
            for h in range(HG):
                v(ve.tensor_scalar(seg[:, h, :], bank4[:, h, :], acs_n[:, c, cut(g * HG + h, 1)], 0.0, ALU.subtract, ALU.min), "SEG")
            need(ae, "SEG")
            a(ae.activation(seg[:, :, :], seg[:, :, :], ACT.Exp), "ES")
            need(ae, "CTE")
            a(ae.activation(ec, bank4, ACT.Exp), "bank 4")
            need(ve, "X", "Y", "BX")
            xs = bank[2][:, 0:2 * P].rearrange("p (h q) -> p h q", h=HG)
            by_head = lambda t: t[:, c, heads].unsqueeze(2).broadcast_to([P, HG, HEAD_P])
            v(ve.tensor_tensor(xdt[:, :, :], xs, by_head(dt_n), ALU.mult))
            need(ve, "CB")
            v(ve.tensor_tensor(cbm[:, :], bank[3][:, 0:P], pr.causal01[:, :], ALU.mult), "bank 3")
            need(ve, "ES", "bank 3", "Y")
            v(ve.tensor_tensor(lt[:, :, :], seg[:, :, :], cbm[:, :].unsqueeze(1).broadcast_to([P, HG, P]), ALU.mult), "LT")
            if c:
                need(ve, "bank 4")
                v(ve.tensor_tensor(cte[:, :, :], ec, grp[:, par, 3, cs].unsqueeze(1).broadcast_to([P, HG, P]), ALU.mult), "CTE")
            v(ve.tensor_tensor(xde[:, :, :], xs, by_head(dte_n), ALU.mult))
            v(ve.tensor_copy(nat[:, :], bank[2][:, 2 * P:3 * P]), "bank 2")

        def chunk_outputs(g, par, c):
            cs = slice(c * P, (c + 1) * P)
            need(te, "LT", "CTE", "S")
            if c == 0:
                need(te, "bank 5", "bank 6")
            for h in range(HG):
                e = (h % 2) * HEAD_P
                o = bank[5 + h // 2][e:e + HEAD_P, cs]
                if c:
                    te.matmul(o, state[:, h, :], cte[:, h, :], start=True, stop=False)
                ins = te.matmul(o, xdt[:, h, :], lt[:, h, :], start=c == 0, stop=True)
            done("Y", ins)
            if c < NT - 1:
                need(te, "bank 7", "bank 2")
                done("BX", te.matmul(bank[7][:, 0:2 * P], nat[:, :], xde[:, :, :].rearrange("p a b -> p (a b)"), start=True, stop=True))

        def chunk_state(g, c):
            bx = bank[7][:, 0:2 * P].rearrange("p (h q) -> p h q", h=HG)
            need(ve, "BX", "Y")
            if c == 0:
                v(ve.tensor_copy(state[:, :, :], bx), "bank 7")
            else:
                v(ve.tensor_tensor(state[:, :, :], state[:, :, :], cd_all[:, c, cut(g * HG, HG)].unsqueeze(2).broadcast_to([P, HG, HEAD_P]), ALU.mult))
                need(ve, "dve")
                v(ve.tensor_tensor(state[:, :, :], state[:, :, :], bx, ALU.add), "bank 7")
            need(te, "bank 7")
            need(ve, "bank 7")

        def gate(g, par):
            for j in range(2):
                need(ve, "Y", "load small", f"y hi {j}")
                v(ve.scalar_tensor_tensor(yy[:, j, :], grp[:, par, j, :], dcol[:, cut(2 * g + j, 1)], bank[5 + j][:, :], ALU.mult, ALU.add), f"bank {5 + j}")
                need(ve, f"bank {5 + j}")
                v(ve.tensor_tensor(yy[:, j, :], yy[:, j, :], grp[:, par, 4 + j, :], ALU.mult), "gated")
            need(ae, "gated", "ES", "LT", "ones read")
            for j in range(2):
                a(ae.activation((lt, seg)[j][:, :, :].rearrange("p a b -> p (a b)"), yy[:, j, :], ACT.Square), "square")
            need(te, "square", "bank 3", "Y")
            te.matmul(bank[3][:, :], pr.ones[:, :], lt[:, :, :].rearrange("p a b -> p (a b)"), start=True, stop=False)
            done("ones read", te.matmul(bank[3][:, :], pr.ones[:, :], seg[:, :, :].rearrange("p a b -> p (a b)"), start=False, stop=True))

        def output(g):
            need(ae, "ones read", "scaled")
            a(ae.activation(pr.nr[:, :], bank[3][:, :], ACT.Ln, bias=pr.eps[:, 0:1], scale=1.0 / (2 * P)), "bank 3")
            need(ae, "bank 3")
            a(ae.activation(pr.nr[:, :], pr.nr[:, :], ACT.Exp, scale=-0.5), "inverse rms")
            for j in range(2):
                need(ve, "inverse rms", "gated", "square")
                v(ve.scalar_tensor_tensor(yy[:, j, :], yy[:, j, :], pr.col("ssm_norm_w", 2 * g + j), pr.nr[:, :], ALU.mult, ALU.mult), "scaled")
                need(ae, "scaled")
                a(ae.activation(y_hi[:, cut(2 * g + j, 1), :], yy[:, j, :].unsqueeze(1), ACT.Copy), f"y hi {j}")
                need(ve, f"y hi {j}")
                v(ve.tensor_tensor(y_lo[:, cut(2 * g + j, 1), :], yy[:, j, :].unsqueeze(1), y_hi[:, cut(2 * g + j, 1), :].bitcast(F32), ALU.subtract), "y lo")
            need(ve, "y lo")

        def step(g, par, following=True):
            for s in range(6):
                if 1 <= s <= 4:
                    chunk_outputs(g, par, s - 1)
                if s < 4:
                    chunk_products(g, par, s)
                if following:
                    unit = project(g + 1, s, s % 2)
                if 1 <= s <= 3:
                    chunk_state(g, s - 1)
                if s < 4:
                    chunk_decays(g, par, s)
                if s == 4:
                    gate(g, par)
                if s == 5:
                    output(g)
                if following and 1 <= s <= 4:
                    convolve(g + 1, 1 - par, s - 1, 1 - s % 2)
                if following:
                    take(1 - par, s, s % 2, unit)

        for n in range(6):
            take(0, n, n % 2, project(0, n, n % 2))
            if n < 4:
                convolve(0, 0, n, n % 2)
        with pr.sig.turns(GROUPS // 2 - 1) as i:
            step(i * 2, 0)
            step(i * 2 + 1, 1)
        step(GROUPS - 2, 0)
        step(GROUPS - 1, 1, following=False)

        pr.settle()
        pr.clear_squares()
        need(te, "y hi 0", "y hi 1", "y lo")
        with pr.sig.turns(KD // 2) as m2:
            for e in range(2):
                m = m2 * 2 + e
                for part in range(2):
                    unit = pr.unit([(w_out[part * D:(part + 1) * D, cut(m * P, P)], 0)], KD, [e],
                                   lambda k: (y_hi[:, part * KD + k, :], y_lo[:, part * KD + k, :]), start=part == 0, stop=part == 1)
                pr.residual(m, e, unit, 1.0, True)


class Attention:

    def __init__(self, pr, slots, window=False):
        self.pr, self.window = pr, window
        self.diag = pr.sb("diag", [P, slots, 2, NT, P], F32R)
        self.prob = pr.sb("prob", [P, slots, 10 * P])
        self.top = pr.sb("top", [P, slots, NT])
        self.top_hi = pr.sb("top_hi", [P, slots, NT], F32R)
        self.top_lo = pr.sb("top_lo", [P, slots, NT])
        self.sink_exp = pr.sb("sink_exp", [1, slots, T]) if window else None

    def place(self, t, n):
        if self.window:
            return t // 2, t % 2 * 2 * P
        return {4: (0, 0), 3: (1, 0), 1: (1, 3 * P), 2: (2, 0)}[n]

    def keys(self, i):
        return (max(i - 1, 0), min(i + 1, 2)) if self.window else (0, i + 1)

    def queries(self, j):
        return (j, min(NT - j, 2)) if self.window else (j, NT - j)

    def by_bank(self, blocks):
        tiles = {}
        for t in range(NT):
            tiles.setdefault(self.place(t, blocks(t)[1])[0], []).append(t)
        return sorted(tiles.items())

    def product(self, out, terms):
        for n, (w, x, c) in enumerate(terms):
            to = out[:, c:c + x.shape[-1]]
            ins = self.pr.te.matmul(to, w, x, start=n == 0, stop=n == len(terms) - 1)
        return ins

    def scores(self, slot, banks, q, k, extra, sink=None):
        pr = self.pr
        te, ve, need, v, done = pr.te, pr.ve, pr.need, pr.v, pr.done
        block = lambda i, n: pr.bank[banks[b]][:, cut(self.place(i, n)[1], n * P)]
        for b, tiles in self.by_bank(self.keys):
            need(te, f"bank {banks[b]}")
            for i in tiles:
                j, n = self.keys(i)
                ins = self.product(block(i, n), [(q(i, i + 1), k(j, j + n), 0)] + extra(j, n))
            done(f"S {slot}", ins)
            need(ve, f"S {slot}", f"diag {slot}")
            for i in tiles:
                v(ve.tensor_reduce(self.top[:, slot, i:i + 1], block(i, self.keys(i)[1]), AX, ALU.max), f"bank {banks[b]}")
        need(ve, *(f"bank {banks[b]}" for b, _ in self.by_bank(self.keys)))
        top, hi, lo = (t[:, slot, :] for t in (self.top, self.top_hi, self.top_lo))
        if sink is not None:
            v(ve.tensor_tensor(top, top, sink.broadcast_to([P, NT]), ALU.max))
            need(ve, "dve")
        v(ve.tensor_scalar(hi, top, -1.0, None, ALU.mult))
        need(ve, "dve")
        v(ve.scalar_tensor_tensor(lo, top, -1.0, hi.bitcast(F32), ALU.mult, ALU.subtract))
        full = [P, NT, P]
        need(ve, "dve", f"ST {slot}")
        for n, t in enumerate((hi.bitcast(F32), lo)):
            v(ve.tensor_tensor(self.diag[:, slot, n], pr.ident[:, :].unsqueeze(1).broadcast_to(full), t.unsqueeze(2).broadcast_to(full), ALU.mult),
              f"diag {slot}")

    def weights(self, slot, banks, q, k, extra, scale=1.0, bias=None, sink=None):
        pr = self.pr
        te, ae, need, a, done = pr.te, pr.ae, pr.need, pr.a, pr.done
        less_top = lambda i, n: [(pr.ones_r[:, :], self.diag[:, slot, half, i:i + n, :].rearrange("p a b -> p (a b)"), 0) for half in range(2)]
        block = lambda j, n: pr.bank[banks[b]][:, cut(self.place(j, n)[1], n * P)]
        need(te, f"diag {slot}")
        need(ae, f"PV {slot}")
        self.prob_at = [sum(self.queries(t)[1] for t in range(j)) * P for j in range(NT)]
        for b, tiles in self.by_bank(self.queries):
            need(te, f"bank {banks[b]}")
            for j in tiles:
                i, n = self.queries(j)
                ins = self.product(block(j, n), [(k(j, j + 1), q(i, i + n), 0)] + less_top(i, n) + extra(n))
            done(f"ST {slot}", ins)
            need(ae, f"ST {slot}")
            for j in tiles:
                n = self.queries(j)[1]
                a(ae.activation(self.prob[:, slot, cut(self.prob_at[j], n * P)], block(j, n), ACT.Exp, scale=scale,
                                bias=0.0 if bias is None else bias(j)), f"bank {banks[b]}")
        if sink is not None:
            need(te, f"bank {banks[2]}")
            done(f"ST {slot}", self.product(pr.bank[banks[2]][:, :], less_top(0, NT)))
            need(ae, f"ST {slot}")
            a(ae.activation(self.sink_exp[:, slot, :], pr.bank[banks[2]][0:1, :], ACT.Exp, bias=sink[0:1, :]), f"bank {banks[2]}")

    def output(self, slot, banks, value, e, dst, sink_value=None):
        pr = self.pr
        te, ve, need, v, done = pr.te, pr.ve, pr.need, pr.v, pr.done
        out = pr.bank[banks[3]]
        need(te, f"bank {banks[3]}", *(f"bank {b}" for b in banks[0:3]))
        if self.window:
            te.matmul(out[:, :], sink_value, self.sink_exp[:, slot, :], start=True, stop=False)
        for j in range(NT):
            i, n = self.queries(j)
            ins = te.matmul(out[:, i * P:(i + n) * P], value(j), self.prob[:, slot, cut(self.prob_at[j], n * P)],
                            start=j == 0 and not self.window, stop=j == NT - 1)
        done(f"PV {slot}", ins)
        rows, others = slice(e * 64, e * 64 + 64), slice(64 - e * 64, 128 - e * 64)
        inverse = pr.nht[rows, slot, :]
        fit = lambda t: t if len(dst.shape) == 2 else t.unsqueeze(1)
        need(ve, f"PV {slot}", f"bank {banks[3]}")
        v(ve.reciprocal(inverse, out[others, :]))
        need(ve, "dve")
        v(ve.tensor_tensor(dst, fit(out[rows, :]), fit(inverse), ALU.mult), f"bank {banks[3]}")


def mla(pr):
    te, ve, ae, ge, se, need, d = pr.te, pr.ve, pr.ae, pr.ge, pr.se, pr.need, pr.d
    v, a, done, bank, sb = pr.v, pr.a, pr.done, pr.bank, pr.sb
    w_in, w_out = d["mla_w_in"][0], d["mla_w_out"][0]
    LQ, LK = Q_LORA // P, KV_LORA // P
    ready = pr.norm_to_h(lambda k: pr.col("norm_w", 4 * KD + k))
    pr.settle()
    with pr.stage():
        o_hi = sb("o_hi", [P, KD, T], F32R)
        o_lo = sb("o_lo", [P, KD, T], F32R)
        wq = sb("wq", [P, LQ, MLA_HEADS * QK])
        wkv = sb("wkv", [P, LK, MLA_HEADS * (NOPE + V_DIM)])
        latent = sb("latent", [P, LQ + LK, T])
        krt = sb("krt", [ROPE, T])
        gain = sb("gain", [P, 2, QK])
        pos = sb("pos", [P, NT])
        pos_i = sb("pos_i", [P, NT], I32)
        freq = sb("freq", [P, HR])
        done("load mla", ae.dma_start(wq[:, :, :], d["mla_w_q_b"][0].rearrange("(k p) m -> p k m", p=P)), 16)
        done("load mla", ae.dma_start(wkv[:, :, :], d["mla_w_kv_b"][0].rearrange("(k p) m -> p k m", p=P)), 16)
        done("load mla", ae.dma_start(gain[:, 0, :], d["mla_q_norm"][0].partition_broadcast(P)), 16)
        done("load mla", ae.dma_start(gain[:, 1, :], d["mla_k_norm"][0].partition_broadcast(P)), 16)
        done("load mla", ae.dma_start(pos_i[:, :], d["positions"].rearrange("a (c p) -> p (a c)", p=P), allow_slow_non_contiguous=True), 16)
        for m in range(LQ + LK + 1):
            b = m % 2
            if m < LQ + LK:
                unit = pr.unit([(w_in[:, m * P:(m + 1) * P], 0)], KD, [b], pr.h, ready=None if m else ready)
                need(ae, unit)
                a(ae.copy(latent[:, m, :], bank[b][:, :]), f"bank {b}")
            else:
                unit = pr.unit([(w_in[:, m * P:m * P + ROPE], 0), (w_in[:, 0:P - ROPE], ROPE)], KD, [b], pr.h)
                need(ae, unit)
                a(ae.copy(krt[:, :], bank[b][0:ROPE, :]), f"bank {b}")
        pr.settle()
        stage_base, pr.base = pr.base, pr.h_at
        cqn = sb("cqn", [P, LQ + LK, T])
        cos = sb("cos", [P, NT, HR])
        sin = sb("sin", [P, NT, HR])
        qc = sb("qc", [P, NT, QK])
        kc = sb("kc", [P, NT, QK])
        vst = sb("vst", [P, NT, V_DIM])
        vn = sb("vn", [P, NT, 3, V_DIM])
        qt = sb("qt", [QK, T])
        kt = sb("kt", [QK, T])
        t4 = sb("t4", [P, 4, NT, HR])
        attention = Attention(pr, 1)
        assert pr.base <= pr.h_end
        pr.base = stage_base
        sq, ot = pr.nsq, pr.nacc
        ss = sb("ss", [P, 3 * NT])
        rr = sb("rr", [P, 3 * NT])

        for k0, n, name in ((0, LQ, "q_a"), (LQ, LK, "kv_a")):
            pr.inverse_rms([latent[:, k0 + k, :] for k in range(n)], n * P, 7, "bank 0")
            need(ve, "inverse rms")
            for k in range(n):
                v(ve.scalar_tensor_tensor(cqn[:, k0 + k, :], latent[:, k0 + k, :], pr.col(name, k), pr.nr[:, :], ALU.mult, ALU.mult), "scaled")

        import numpy as np
        inv_freq = np.float32(1.0) / np.float32(10000.0) ** (np.arange(0, ROPE, 2, dtype=np.float32) / np.float32(ROPE))
        for n in range(HR):
            v(ve.memset(freq[:, n:n + 1], float(inv_freq[n])))
        need(ve, "load mla", "dve")
        v(ve.tensor_copy(pos[:, :], pos_i[:, :]))
        need(ve, "dve")
        angle, turns = t4[:, 0], t4[:, 1]
        full = [P, NT, HR]
        chain = lambda ins: (v(ins), need(ve, "dve"))
        chain(ve.tensor_tensor(angle, pos[:, :].unsqueeze(2).broadcast_to(full), freq[:, :].unsqueeze(1).broadcast_to(full), ALU.mult))
        chain(ve.tensor_scalar(turns, angle, 1.0 / (2 * PI), 12582912.0, ALU.mult, ALU.add))
        chain(ve.tensor_scalar(turns, turns, -12582912.0, None, ALU.add))
        chain(ve.scalar_tensor_tensor(angle, turns, -TWO_PI_HI, angle, ALU.mult, ALU.add))
        chain(ve.scalar_tensor_tensor(angle, turns, -TWO_PI_LO, angle, ALU.mult, ALU.add))
        chain(ve.tensor_scalar(sin[:, :, :], angle, 3.1415925, -3.1415925, ALU.min, ALU.max))
        chain(ve.tensor_scalar(angle, angle, PI / 2, None, ALU.add))
        chain(ve.tensor_scalar(turns, angle, PI, -2 * PI, ALU.is_gt, ALU.mult))
        chain(ve.tensor_tensor(angle, angle, turns, ALU.add))
        chain(ve.tensor_scalar(cos[:, :, :], angle, 3.1415925, -3.1415925, ALU.min, ALU.max))
        need(ae, "dve")
        a(ae.activation(sin[:, :, :], sin[:, :, :], ACT.Sin), "angles")
        a(ae.activation(cos[:, :, :], cos[:, :, :], ACT.Sin), "angles")
        need(ve, "angles")

        def rotate(x, name):
            x1, x2 = x[:, :, 0:HR], x[:, :, HR:ROPE]
            for n, (half, table) in enumerate(((x1, cos), (x2, sin), (x2, cos), (x1, sin))):
                done("rotate", ge.tensor_tensor(t4[:, n], half, table[:, :, :], ALU.mult))
            need(ge, "rotate")
            done(name, ge.tensor_tensor(x1, t4[:, 0], t4[:, 1], ALU.subtract))
            done(name, ge.tensor_tensor(x2, t4[:, 2], t4[:, 3], ALU.add))
            need(ge, name)

        def inverse(cols, n, ready):
            need(ae, ready)
            a(ae.activation(rr[:, 0:cols], ss[:, 0:cols], ACT.Ln, scale=1.0 / n, bias=pr.eps[:, 0:1]))
            need(ae, "act")
            a(ae.activation(rr[:, 0:cols], rr[:, 0:cols], ACT.Exp, scale=-0.5), "rr")

        need(te, "bank 1", "bank 2")
        for tt in range(NT):
            ins = te.transpose(bank[2][:, tt * ROPE:(tt + 1) * ROPE], krt[:, tt * P:(tt + 1) * P], pr.ident[0:ROPE, 0:ROPE])
        done("pe", ins)
        k_rope = bank[2][:, 0:NT * ROPE].rearrange("p (a b) -> p a b", a=NT)
        sq4 = sq[:, :, :].rearrange("p a b -> p (a b)")
        need(ae, "pe", "scaled")
        squares = sq4[:, 0:NT * ROPE].rearrange("p (a b) -> p a b", a=NT)
        a(ae.activation(squares, k_rope, ACT.Square), "sq q")
        need(ve, "sq q")
        v(ve.tensor_reduce(ss[:, 0:NT], squares, AX, ALU.add), "sums")
        inverse(NT, ROPE, "sums")
        need(ve, "rr")
        kr = kc[:, :, NOPE:QK]
        v(ve.tensor_tensor(kr, k_rope, rr[:, 0:NT].unsqueeze(2).broadcast_to([P, NT, ROPE]), ALU.mult), "bank 2")
        need(ve, "bank 2")
        v(ve.tensor_tensor(kr, kr, gain[:, 1, NOPE:QK].unsqueeze(1).broadcast_to([P, NT, ROPE]), ALU.mult))
        need(ge, "dve", "angles", "load mla")
        rotate(kr, "kc")
        for part in range(3):
            done("vn", ge.memset(vn[:, :, part, :], 1.0))
        need(te, "scaled", "load mla", "kc")

        q_bank = bank[0][:, 0:NT * QK].rearrange("p (a b) -> p a b", a=NT)
        kv_bank = bank[1][:, :].rearrange("p (a b) -> p a b", a=NT)
        q_sq = sq4[:, 0:NT * QK].rearrange("p (a b) -> p a b", a=NT)
        k_sq = sq4[:, T:T + NT * NOPE].rearrange("p (a b) -> p a b", a=NT)

        def project(h):
            for b, k0, n, w, width, name in ((q_bank, 0, LQ, wq, QK, "q"), (kv_bank, LQ, LK, wkv, NOPE + V_DIM, "kv")):
                need(te, "bank 0" if name == "q" else "bank 1", "sq q", "sq k", "v stored")
                for tt in range(NT):
                    for k in range(n):
                        ins = te.matmul(b[:, tt, :], cqn[:, k0 + k, tt * P:(tt + 1) * P], w[:, k, cut(h * width, width)],
                                        start=k == 0, stop=k == n - 1)
                done("pe " + name, ins)
            need(ae, "pe q", "sums")
            a(ae.activation(q_sq, q_bank, ACT.Square), "sq q")
            need(ae, "pe kv", "vn")
            a(ae.activation(k_sq, kv_bank[:, :, 0:NOPE], ACT.Square), "sq k")
            a(ae.copy(vst[:, :, :], kv_bank[:, :, NOPE:]), "v stored")
            need(ve, "sq q", "sq k", "rr")
            v(ve.tensor_reduce(ss[:, 0:NT], q_sq[:, :, 0:NOPE], AX, ALU.add), "sums")
            v(ve.tensor_reduce(ss[:, NT:2 * NT], q_sq[:, :, NOPE:QK], AX, ALU.add), "sums")
            v(ve.tensor_reduce(ss[:, 2 * NT:3 * NT], k_sq, AX, ALU.add), "sums")
            need(ve, "sums")
            v(ve.tensor_scalar(ss[:, NT:2 * NT], ss[:, NT:2 * NT], float(NOPE // ROPE), None, ALU.mult), "sums")

        def normalise():
            by = lambda n, width: rr[:, n * NT:(n + 1) * NT].unsqueeze(2).broadcast_to([P, NT, width])
            need(ve, "rr", "turned q", "turned k")
            v(ve.tensor_tensor(qc[:, :, 0:NOPE], q_bank[:, :, 0:NOPE], by(0, NOPE), ALU.mult), "bank 0")
            v(ve.tensor_tensor(qc[:, :, NOPE:QK], q_bank[:, :, NOPE:QK], by(1, ROPE), ALU.mult), "bank 0")
            v(ve.tensor_tensor(kc[:, :, 0:NOPE], kv_bank[:, :, 0:NOPE], by(2, NOPE), ALU.mult), "bank 1")
            need(ae, "bank 0", "bank 1")
            need(ge, "bank 0", "bank 1")
            done("qc", ge.tensor_tensor(qc[:, :, :], qc[:, :, :], gain[:, 0, :].unsqueeze(1).broadcast_to([P, NT, QK]), ALU.mult))
            done("kc", ge.tensor_tensor(kc[:, :, 0:NOPE], kc[:, :, 0:NOPE], gain[:, 1, 0:NOPE].unsqueeze(1).broadcast_to([P, NT, NOPE]), ALU.mult))
            need(ge, "qc")
            rotate(qc[:, :, NOPE:QK], "qc")

        def keep_values(e):
            need(ge, "v stored", "PV 0")
            done("vn", ge.tensor_copy(vn[:, :, 2 * e, :], vst[:, :, :]))

        def turn():
            for t, name, b in ((kc, "k", 3), (qc, "q", 2)):
                need(te, name + "c", f"bank {b}")
                for tt in range(NT):
                    ins = te.transpose(bank[b][0:QK, tt * P:(tt + 1) * P], t[:, tt, :], pr.ident[:, :])
                done("turned " + name, ins)
            need(ae, "turned k", "ST 0")
            a(ae.copy(kt[:, :], bank[3][0:QK, :]), "bank 3")
            need(ve, "turned q", "ST 0")
            v(ve.tensor_copy(qt[:, :], bank[2][0:QK, :]), "bank 2")

        banks = (4, 5, 6, 7)
        q = lambda i, j: qt[:, i * P:j * P]
        k = lambda i, j: kt[:, i * P:j * P]

        def output(e, pair):
            rows = slice(e * V_DIM, (e + 1) * V_DIM)
            need(te, "vn")
            need(ve, "o hi", "o lo")
            attention.output(0, banks, lambda j: vn[:, j, e:e + 2, :].rearrange("p a b -> p (a b)"), e, ot[rows, :])
            if e:
                need(ae, "bank 7")
                a(ae.activation(o_hi[:, cut(pair, 1), :], ot[:, :].unsqueeze(1), ACT.Copy), "o hi")
                need(ge, "o hi", "bank 7")
                done("o lo", ge.tensor_tensor(o_lo[:, cut(pair, 1), :], ot[:, :].unsqueeze(1), o_hi[:, cut(pair, 1), :].bitcast(F32), ALU.subtract))

        def head(h, e, pair=None):
            further = isinstance(h, int)
            if not further or h + 1 < MLA_HEADS:
                normalise()
            need(te, "bank 2", "bank 3")
            attention.scores(0, banks, q, k, pr.mask_keys)
            if pair is not None:
                output(1 - e, pair)
            if not further or h + 1 < MLA_HEADS:
                keep_values(1 - e)
            if not further or h + 2 < MLA_HEADS:
                project(h + 2)
            attention.weights(0, banks, q, k, pr.mask_queries, scale=QK ** -0.5)
            if not further or h + 2 < MLA_HEADS:
                inverse(3 * NT, NOPE, "sums")
            if not further or h + 1 < MLA_HEADS:
                turn()

        ae.preload_act_table_set("natural_log_exp_and_others")
        project(0)
        inverse(3 * NT, NOPE, "sums")
        normalise()
        keep_values(0)
        turn()
        project(1)
        inverse(3 * NT, NOPE, "sums")
        head(0, 0)
        with pr.sig.turns((MLA_HEADS - 4) // 2) as i:
            head(i * 2 + 1, 1, i)
            head(i * 2 + 2, 0, i)
        for h in range(MLA_HEADS - 3, MLA_HEADS):
            head(h, h % 2, (h - 1) // 2)
        output(1, MLA_HEADS // 2 - 1)
        need(te, "o hi", "o lo")
        need(ve, "o lo")
        out_projection(pr, w_out, o_hi, o_lo, lambda m: 1.0)


def out_projection(pr, w, y_hi, y_lo, gate):
    pr.settle()
    pr.clear_squares()
    with pr.sig.turns(KD // 2) as m2:
        for e in range(2):
            m = m2 * 2 + e
            unit = pr.unit([(w[:, cut(m * P, P)], 0)], KD, [e], lambda k: (y_hi[:, k, :], y_lo[:, k, :]))
            pr.residual(m, e, unit, gate(m), True)


def mixer(pr):
    te, ve, ae, ge, se, need, d = pr.te, pr.ve, pr.ae, pr.ge, pr.se, pr.need, pr.d
    v, a, done, bank, sb = pr.v, pr.a, pr.done, pr.bank, pr.sb
    w_in, w_out = d["w_in_2"][0], d["w_out_2"][0]
    Q_A, K_A, V_A, X_B, G_B, Q_C, K_C, V_C, N_TILES = 0, 4, 5, 6, 8, 10, 12, 14, 16
    LB = 32
    ready = pr.norm_to_h(lambda k: pr.mod[:, 8 + k:9 + k], lambda k: pr.mod[:, k:k + 1])
    pr.settle()
    with pr.stage():
        stage_start = pr.base
        proj = sb("proj", [P, N_TILES, T])
        y = sb("y", [P, KD, T])
        f_t = sb("f_t", [FOX_HEADS, T])
        bf = sb("bf", [FOX_HEADS, 1])
        sinks = sb("sinks", [P, SWA_HEADS])
        neg_slope = sb("neg_slope", [P, SWA_HEADS])
        gates = sb("gates", [P, 2, 2, P])
        dist = sb("dist", [P, 2, 2 * P])
        window = sb("window", [P, 2, 2 * P])
        done("gates set", ge.memset(gates[:, :, :, :], 0.0))
        done("window set", ge.memset(window[:, :, :], 0.0))
        for n, (start, step) in enumerate(((P, -1), (0, 1))):
            done("window set", ge.iota(dist[:, n, :], pattern=[[step, 2 * P]], base=start, channel_multiplier=-step,
                                       allow_small_or_imprecise_dtypes=True))
            for sign, base in ((1, start), (-1, P - 1 - start)):
                need(ge, "window set")
                done("window set", ge.affine_select(out=window[:, n, :], in_=window[:, n, :], compare_op=ALU.is_ge, fill=NEG, base=base,
                                                    pattern=[[sign * step, 2 * P]], channel_multiplier=-sign * step))
        for h in range(SWA_HEADS):
            v(ve.memset(neg_slope[:, h:h + 1], -2.0 ** (-8.0 * (h + 1) / SWA_HEADS)), "slopes")
        done("load mixer", ae.dma_start(bf[:, :], d["fox_bf_2"].rearrange("a h -> h a")), 16)
        done("load mixer", ae.dma_start(sinks[:, :], d["sinks_2"][0].partition_broadcast(P)), 16)
        need(ae, "gates set")
        for n, w in enumerate(("lru_wa_2", "lru_wx_2")):
            for blk in range(LRU // LB):
                q = blk % (P // LB) * LB
                done("load gates", ae.dma_start(gates[q:q + LB, n, blk * LB // P, q:q + LB], d[w][0, blk]), 16)

        for j in range(4):
            unit = pr.unit([(w_in[:, j * HEAD_DIM:(j + 1) * HEAD_DIM], 0), (w_in[:, (j + 4) * HEAD_DIM:(j + 5) * HEAD_DIM], HEAD_DIM)],
                           KD, [j % 2], pr.h, ready=None if j else ready)
            need(ae, unit)
            a(ae.copy(proj[:, j, :], bank[j % 2][:, :]), f"bank {j % 2}")
        with pr.sig.turns((N_TILES - K_A) // 2) as i:
            for e in range(2):
                j = i * 2 + (K_A + e)
                unit = pr.unit([(w_in[:, cut(j * P, P)], 0)], KD, [e], pr.h)
                need(ae, unit)
                a(ae.copy(proj[:, cut(j, 1), :], bank[e][:, :].unsqueeze(1)), f"bank {e}")
        unit = pr.unit([(w_in[:, N_TILES * P:N_TILES * P + FOX_HEADS], 0), (w_in[:, 0:P - FOX_HEADS], FOX_HEADS)], KD, [0], pr.h)
        need(ve, unit, "load mixer")
        v(ve.tensor_scalar(f_t[:, :], bank[0][0:FOX_HEADS, :], bf[:, 0:1], -1.0, ALU.add, ALU.mult), "bank 0")
        pr.settle()

        stage_base, pr.base = pr.base, pr.h_at
        attention = Attention(pr, 2, window=True)
        values_a = sb("values_a", [P, SWA_KV, NT, 3, HEAD_DIM])
        fox_values = sb("fox_values", [P, NT, 3, HEAD_DIM])
        assert pr.base <= pr.h_end, pr.base - pr.h_end
        pr.base = stage_base
        qs = sb("qs", [P, T])
        ks = sb("ks", [P, T])
        values_c = sb("values_c", [P, 2, NT, P])
        csp = sb("csp", [FOX_HEADS, T])
        csp_hi = sb("csp_hi", [FOX_HEADS, T], F32R)
        csp_lo = sb("csp_lo", [FOX_HEADS, T], F32R)
        csp_n = sb("csp_n", [P, NT, FOX_HEADS])
        csp_pair = sb("csp_pair", [P, NT, 2])
        tmp = [sb("tmp", [P, T]) for _ in range(4)]
        sel = sb("sel", [FOX_HEADS, 2, P], F32R)
        bias = sb("bias", [P, SWA_KV, 2, 2 * P], F32R)
        sink = sb("sink", [P, SWA_KV])
        sink_value = sb("sink_value", [1, 3, HEAD_DIM])
        ones_row = sb("ones_row", [FOX_HEADS, T])
        u = sb("u", [P, CONV_K - 1 + T])
        xc = sb("xc", [P, T])

        for t in (values_a, fox_values, sink_value):
            v(ve.memset(t[tuple(slice(None) for _ in t.shape)], 1.0), "values set")
        need(ve, "values set")
        v(ve.memset(sink_value[:, 1, :], 0.0), "values set")
        for n, tile in enumerate((V_A, V_C, V_C + 1)):
            need(te, f"bank {n}")
            for tt in range(NT):
                ins = te.transpose(bank[n][:, tt * P:(tt + 1) * P], proj[:, tile, tt * P:(tt + 1) * P], pr.ident[:, :])
            done("pe", ins)
            need(ve, "pe")
            turned = bank[n][:, :].rearrange("p (a b) -> p a b", a=NT)
            if n:
                v(ve.tensor_copy(values_c[:, n - 1], turned), f"bank {n}")
            else:
                for kv in range(SWA_KV):
                    v(ve.tensor_copy(values_a[:, kv, :, 1, :], turned[:, :, kv * HEAD_DIM:(kv + 1) * HEAD_DIM]), f"bank {n}")

        rows = lambda t: t[0:FOX_HEADS, :]
        softplus(pr, rows(xc), f_t[:, :], (rows(tmp[0]), rows(tmp[1]), rows(tmp[2])), FOX_HEADS, "bank 0", "softplus")
        need(ve, "softplus")
        v(ve.memset(ones_row[:, :], 1.0))
        need(ve, "dve")
        v(ve.tensor_tensor_scan(csp[:, :], ones_row[:, :], rows(xc), 0.0, ALU.mult, ALU.add), "csp")
        need(ve, "csp")
        v(ve.tensor_copy(csp_hi[:, :], csp[:, :]), "csp hi")
        need(ve, "csp hi")
        v(ve.tensor_tensor(csp_lo[:, :], csp[:, :], csp_hi[:, :].bitcast(F32), ALU.subtract), "csp lo")
        need(te, "csp", "bank 3")
        for tt in range(NT):
            ins = te.transpose(bank[3][:, tt * FOX_HEADS:(tt + 1) * FOX_HEADS], csp[:, tt * P:(tt + 1) * P], pr.ident[0:FOX_HEADS, 0:FOX_HEADS])
        done("pe", ins)
        need(ve, "pe")
        v(ve.tensor_copy(csp_n[:, :, :].rearrange("p a b -> p (a b)"), bank[3][:, 0:NT * FOX_HEADS]), "bank 3")

        lam = sb("lam", [P, 6])
        need(ve, "cols")
        v(ve.tensor_scalar(lam[:, 2:4], pr.col("lru_lam", 0, 2), -1.0, None, ALU.mult), "lam")
        softplus(pr, lam[:, 0:2], lam[:, 2:4], (lam[:, 4:6], tmp[0][:, 0:2], tmp[0][:, 2:4]), P, "lam", "decay rate")
        need(ve, "decay rate")
        v(ve.tensor_scalar(lam[:, 0:2], lam[:, 0:2], -LRU_C, None, ALU.mult), "decay rate")
        v(ve.memset(u[:, 0:CONV_K - 1], 0.0), "u set")
        rg, ig, la, sc = (t[:, :] for t in tmp)
        for k in range(2):
            need(ae, "u set", "lru conv")
            a(ae.copy(u[:, CONV_K - 1:], proj[:, X_B + k, :]), "u set")
            need(ve, "u set", "lru gates", "lru")
            v(ve.tensor_scalar(xc[:, :], u[:, CONV_K - 1:], pr.col("conv_w_2", 6 + k), pr.col("conv_b_2", k), ALU.mult, ALU.add))
            for c in range(CONV_K - 1):
                need(ve, "dve", "lru conv")
                v(ve.scalar_tensor_tensor(xc[:, :], u[:, c:c + T], pr.col("conv_w_2", 2 * c + k), xc[:, :], ALU.mult, ALU.add), "lru conv")
            need(te, "lru conv", "load gates", "bank 0", "bank 1")
            te.matmul(bank[0][:, :], gates[:, 0, k, :], xc[:, :], start=True, stop=True)
            done("lru gates", te.matmul(bank[1][:, :], gates[:, 1, k, :], xc[:, :], start=True, stop=True))
            need(ae, "lru gates", "lru")
            a(ae.activation(rg, bank[0][:, :], ACT.Sigmoid, bias=pr.col("lru_ba", k)), "bank 0")
            a(ae.activation(ig, bank[1][:, :], ACT.Sigmoid, bias=pr.col("lru_bx", k)), "bank 1")
            need(ve, "bank 0", "bank 1", "decay rate", "lru conv")
            v(ve.tensor_scalar(la, rg, lam[:, k:k + 1], None, ALU.mult), "log a")
            v(ve.tensor_tensor(ig, ig, xc[:, :], ALU.mult), "gated x")
            need(ae, "log a")
            a(ae.activation(rg, la, ACT.Exp), "lru a")
            a(ae.activation(sc, la, ACT.Exp, scale=2.0))
            a(ae.activation(la, la, ACT.Tanh), "lru tanh")
            need(ve, "lru tanh", "gated x")
            v(ve.scalar_tensor_tensor(sc, sc, 1.0, la, ALU.add, ALU.mult), "one less a2")
            need(ae, "one less a2")
            a(ae.activation(sc, sc, ACT.Sqrt, scale=-1.0), "root")
            a(ae.activation(la, proj[:, G_B + k, :], ACT.Gelu_apprx_tanh), "gelu")
            need(ve, "root")
            v(ve.tensor_tensor(ig, ig, sc, ALU.mult))
            need(ve, "dve")
            v(ve.tensor_tensor_scan(sc, rg, ig, 0.0, ALU.mult, ALU.add))
            need(ve, "dve", "gelu")
            v(ve.tensor_tensor(y[:, 4 + k, :], sc, la, ALU.mult), "lru")

        pr.settle()
        ae.preload_act_table_set("natural_log_exp_and_others")
        need(ve, "slopes", "load mixer", "window set")
        scale = HEAD_DIM ** -0.5
        flat = lambda t: t.rearrange("p a b -> p (a b)")
        slot_banks = ((4, 5, 6, 7), (0, 1, 2, 3))
        qt = lambda rows: lambda i, j: qs[rows, i * P:j * P]
        halves = [slice(n * HEAD_DIM, (n + 1) * HEAD_DIM) for n in range(2)]
        with pr.sig.turns(2) as i:
            for e in range(2):
                need(ve, "ST 0", "ST 1")
                v(ve.tensor_scalar(qs[:, :], flat(proj[:, cut(i * 2 + e, 1), :]), scale, None, ALU.mult), "qs")
                for kv in range(SWA_KV):
                    h = i * 2 + (e + 4 * kv)
                    v(ve.scalar_tensor_tensor(bias[:, kv], dist[:, :, :], neg_slope[:, cut(h, 1)], window[:, :, :], ALU.mult, ALU.add), "qs")
                    need(ve, f"bank {slot_banks[kv][2]}")
                    v(ve.tensor_copy(sink[:, kv:kv + 1], sinks[:, cut(h, 1)]), "qs")
                need(te, "qs")
                need(ve, "qs")
                need(ae, "qs")
                kt = lambda rows: lambda i, j: proj[rows, K_A, i * P:j * P]
                for kv in range(SWA_KV):
                    attention.scores(kv, slot_banks[kv], qt(halves[kv]), kt(halves[kv]),
                                     lambda j, n: [(pr.ident_r[:, :], bias[:, kv, 0, (2 - n) * P:], 0)], sink=sink[:, kv:kv + 1])
                for kv in range(SWA_KV):
                    attention.weights(kv, slot_banks[kv], qt(halves[kv]), kt(halves[kv]),
                                      lambda n: [(pr.ident_r[:, :], bias[:, kv, 1, 0:n * P], 0)], sink=sink[:, kv:kv + 1])
                for kv in range(SWA_KV):
                    beside = slice(1 - e, 3 - e)
                    attention.output(kv, slot_banks[kv], lambda j: flat(values_a[:, kv, j, beside, :]), e,
                                     y[halves[e], cut(i + 2 * kv, 1), :], sink_value=flat(sink_value[:, beside, :]))

        attention.window = False
        with pr.sig.turns(FOX_HEADS // 2) as i:
            need(ve, "ST 0", "ST 1", "PV 0", "PV 1", "bank 4", "bank 5", "bank 6", "bank 0", "bank 1", "bank 2")
            v(ve.tensor_scalar(qs[:, :], flat(proj[:, cut(Q_C + i, 1), :]), scale, None, ALU.mult), "qs")
            v(ve.tensor_copy(ks[:, :], flat(proj[:, cut(K_C + i, 1), :])), "qs")
            v(ve.tensor_copy(fox_values[:, :, 0, :], values_c[:, cut(i, 1), :, 0:HEAD_DIM].rearrange("p c a b -> p (c a) b")), "qs")
            v(ve.tensor_copy(fox_values[:, :, 2, :], values_c[:, cut(i, 1), :, HEAD_DIM:].rearrange("p c a b -> p (c a) b")), "qs")
            v(ve.tensor_copy(sel[:, :, :], pr.ident[0:FOX_HEADS, cut(i * 2, 2)].unsqueeze(2).broadcast_to([FOX_HEADS, 2, P])), "qs")
            v(ve.tensor_copy(csp_pair[:, :, :], csp_n[:, :, cut(i * 2, 2)]), "qs")
            need(te, "qs")
            need(ae, "qs")
            kt = lambda rows: lambda i, j: ks[rows, i * P:j * P]
            for e in range(2):
                attention.scores(e, slot_banks[e], qt(halves[e]), kt(halves[e]), lambda j, n: pr.mask_keys(j, n) + [
                    (sel[:, e, :], part[:, j * P:(j + n) * P], 0) for part in (csp_hi, csp_lo)])
            for e in range(2):
                attention.weights(e, slot_banks[e], qt(halves[e]), kt(halves[e]), pr.mask_queries, bias=lambda j: csp_pair[:, j, e:e + 1])
            for e in range(2):
                attention.output(e, slot_banks[e], lambda j: flat(fox_values[:, j, e:e + 2, :]), e, y[halves[e], cut(i + 6, 1), :])

        pr.settle()
        after, pr.base = pr.base, stage_start
        y_hi = sb("y_hi", [P, KD, T], F32R)
        y_lo = sb("y_lo", [P, KD, T], F32R)
        pr.base = after
        for k0, n in ((0, 4), (4, 2), (6, 2)):
            pr.inverse_rms([y[:, k0 + k, :] for k in range(n)], n * P, 0, "bank 7")
            for k in range(k0, k0 + n):
                t = pr.nht[:, k % 2, :]
                need(ve, "inverse rms", f"h hi {k % 2}", f"h lo {k % 2}")
                v(ve.scalar_tensor_tensor(t, y[:, k, :], pr.col("out_gain", k), pr.nr[:, :], ALU.mult, ALU.mult), "scaled")
                need(ae, "scaled")
                a(ae.activation(y_hi[:, k, :], t, ACT.Copy), f"h hi {k % 2}")
                need(ve, "scaled", f"h hi {k % 2}")
                v(ve.tensor_tensor(y_lo[:, k, :], t, y_hi[:, k, :].bitcast(F32), ALU.subtract), f"h lo {k % 2}")
        out_projection(pr, w_out, y_hi, y_lo, lambda m: pr.mod[:, cut(m + 16, 1)])


def moe(pr):
    te, ve, ae, ge, se, need, d = pr.te, pr.ve, pr.ae, pr.ge, pr.se, pr.need, pr.d
    v, a, done, bank, sb = pr.v, pr.a, pr.done, pr.bank, pr.sb
    wg, wu = (d[n][0].rearrange("e k m -> k e m") for n in ("w_gate_2", "w_up_2"))
    wd = d["w_down_2"][0].rearrange("e k m -> (e k) m")
    NL = N_GROUPS + N_EXPERTS
    ready = pr.norm_to_h(lambda k: pr.mod[:, 32 + k:33 + k], lambda k: pr.mod[:, 24 + k:25 + k])
    pr.settle()
    with pr.stage():
        hid = sb("hid", [P, 4, T])
        g_hi = sb("g_hi", [P, 4, T], F32R)
        g_lo = sb("g_lo", [P, 4, T], F32R)
        comb_t = sb("comb_t", [N_EXPERTS, T])
        sel = sb("sel", [N_EXPERTS, 2, P])
        cb = sb("cb", [P, 2, T])
        act = sb("act", [P, T])
        logits_t = sb("logits_t", [NL, T])
        br = sb("br", [NL, 1])
        lg = sb("lg", [P, NT, NL])
        rank = sb("rank", [P, 4])
        m1 = sb("m1", [P, NT])
        m2 = sb("m2", [P, NT])
        gp = sb("gp", [P, NT])
        e4 = sb("e4", [P, NT, 4])
        t4 = sb("t4", [P, NT, 4])
        group = sb("group", [P, NT, 4])
        first = sb("first", [P, NT, 4])
        second = sb("second", [P, NT, 4])
        inside = sb("inside", [P, NT, 4])
        w4 = sb("w4", [P, NT, 4])
        comb = sb("comb", [P, NT, N_GROUPS, PER_GROUP])
        done("load router", ae.dma_start(br[0:N_GROUPS, :], d["b_router_group_2"].rearrange("a h -> h a")), 16)
        done("load router", ae.dma_start(br[N_GROUPS:NL, :], d["b_router_expert_2"].rearrange("a h -> h a")), 16)
        for n in range(4):
            v(ve.memset(rank[:, n:n + 1], 4.0 - n), "rank")
        unit = pr.unit([(d["w_router_group_2"][0], 0), (d["w_router_expert_2"][0], N_GROUPS), (d["w_gate_2"][0, 0, :, 0:P - NL], NL)],
                       KD, [0], pr.h, ready=ready)
        need(ve, unit, "load router")
        v(ve.tensor_scalar(logits_t[:, :], bank[0][0:NL, :], br[:, 0:1], None, ALU.add), "bank 0")
        need(te, "bank 0", "bank 2")
        for tt in range(NT):
            ins = te.transpose(bank[2][:, tt * NL:(tt + 1) * NL], logits_t[:, tt * P:(tt + 1) * P], pr.ident[0:NL, 0:NL])
        done("pe", ins)
        need(ve, "pe", "rank")
        v(ve.tensor_copy(lg[:, :, :], bank[2][:, 0:NT * NL].rearrange("p (a b) -> p a b", a=NT)), "bank 2")
        need(ve, "bank 2")
        shape = [P, NT, 4]
        wide = lambda t: t[:, :].unsqueeze(2).broadcast_to(shape)
        chain = lambda ins: (v(ins), need(ve, "dve"))

        def argmax(out, x, top):
            chain(ve.tensor_reduce(top[:, :], x, AX, ALU.max))
            chain(ve.tensor_tensor(out[:, :, :], x, wide(top), ALU.is_equal))
            chain(ve.tensor_tensor(out[:, :, :], out[:, :, :], rank[:, :].unsqueeze(1).broadcast_to(shape), ALU.mult))
            chain(ve.tensor_reduce(m2[:, :], out[:, :, :], AX, ALU.max))
            chain(ve.tensor_tensor(out[:, :, :], out[:, :, :], wide(m2), ALU.is_equal))

        groups = lg[:, :, 0:N_GROUPS]
        argmax(group, groups, m1)
        chain(ve.tensor_tensor(e4[:, :, :], groups, wide(m1), ALU.subtract))
        need(ae, "dve")
        a(ae.activation(e4[:, :, :], e4[:, :, :], ACT.Exp))
        need(ve, "act")
        chain(ve.tensor_reduce(gp[:, :], e4[:, :, :], AX, ALU.add))
        for g in range(N_GROUPS):
            own = lg[:, :, N_GROUPS + g * PER_GROUP:N_GROUPS + (g + 1) * PER_GROUP]
            dst = inside if g == 0 else t4
            chain(ve.tensor_tensor(dst[:, :, :], own, group[:, :, g:g + 1].broadcast_to(shape), ALU.mult))
            if g:
                chain(ve.tensor_tensor(inside[:, :, :], inside[:, :, :], t4[:, :, :], ALU.add))
        argmax(first, inside[:, :, :], m1)
        chain(ve.tensor_tensor(e4[:, :, :], inside[:, :, :], wide(m1), ALU.subtract))
        need(ae, "dve")
        a(ae.activation(e4[:, :, :], e4[:, :, :], ACT.Exp))
        need(ve, "act")
        chain(ve.scalar_tensor_tensor(t4[:, :, :], first[:, :, :], NEG, inside[:, :, :], ALU.mult, ALU.add))
        argmax(second, t4[:, :, :], m1)
        chain(ve.tensor_tensor(second[:, :, :], second[:, :, :], first[:, :, :], ALU.add))
        chain(ve.tensor_tensor(w4[:, :, :], e4[:, :, :], second[:, :, :], ALU.mult))
        chain(ve.tensor_reduce(m1[:, :], w4[:, :, :], AX, ALU.add))
        chain(ve.tensor_tensor(m1[:, :], m1[:, :], gp[:, :], ALU.mult))
        chain(ve.reciprocal(m1[:, :], m1[:, :]))
        chain(ve.tensor_tensor(w4[:, :, :], w4[:, :, :], wide(m1), ALU.mult))
        for g in range(N_GROUPS):
            v(ve.tensor_tensor(comb[:, :, g, :], w4[:, :, :], group[:, :, g:g + 1].broadcast_to(shape), ALU.mult), "comb")
        need(te, "comb", "bank 3")
        for tt in range(NT):
            ins = te.transpose(bank[3][0:N_EXPERTS, tt * P:(tt + 1) * P], comb[:, tt, :, :].rearrange("p a b -> p (a b)"), pr.ident[:, :])
        done("pe", ins)
        need(ve, "pe")
        v(ve.tensor_copy(comb_t[:, :], bank[3][0:N_EXPERTS, :]), "bank 3")
        need(ve, "bank 3")

        def experts(i, last=False):
            need(ve, "expert rows")
            v(ve.tensor_copy(sel[:, :, :], pr.ident[0:N_EXPERTS, cut(i * 2, 2)].unsqueeze(2).broadcast_to([N_EXPERTS, 2, P])), "expert sel")
            for e in range(2):
                need(te, "expert sel", f"bank {4 + e}")
                done("expert rows", te.matmul(bank[4 + e][:, :], sel[:, e, :], comb_t[:, :], start=True, stop=True))
                need(ae, "expert rows", "weighted")
                a(ae.copy(cb[:, e, :], bank[4 + e][:, :]), f"bank {4 + e}")
            for n in range(4):
                e, c = n // 2, n % 2 * P
                own = lambda w: w[:, cut(i * 2 + e, 1), c:c + P].rearrange("k e m -> k (e m)")
                gate = pr.unit([(own(wg), 0)], KD, [0], pr.h)
                need(ae, gate, "bank 1")
                a(ae.activation(act[:, :], bank[0][:, :], ACT.Silu), "bank 0")
                up = pr.unit([(own(wu), 0)], KD, [1], pr.h)
                need(ve, up, "bank 0", "g hi", "g lo")
                v(ve.tensor_tensor(hid[:, n, :], act[:, :], bank[1][:, :], ALU.mult), "bank 1")
                need(ve, "bank 1", f"bank {4 + e}")
                v(ve.tensor_tensor(hid[:, n, :], hid[:, n, :], cb[:, e, :], ALU.mult), "weighted")
                need(ae, "weighted")
                a(ae.activation(g_hi[:, n, :], hid[:, n, :], ACT.Copy), "g hi")
                need(ve, "weighted", "g hi")
                v(ve.tensor_tensor(g_lo[:, n, :], hid[:, n, :], g_hi[:, n, :].bitcast(F32), ALU.subtract), "g lo")
            need(te, "g hi", "g lo")
            for q in range(KD // 2):
                unit = pr.unit([(wd[cut(i * 512, 512), q * 256:(q + 1) * 256], 0)], 4, [2, 3], lambda k: (g_hi[:, k, :], g_lo[:, k, :]))
                for e in range(2):
                    m = 2 * q + e
                    pr.residual(m, 2 + e, unit, pr.mod[:, 40 + m:41 + m], squares=last)

        with pr.sig.turns(N_EXPERTS // 2 - 1) as i:
            experts(i)
        pr.clear_squares()
        experts(N_EXPERTS // 2 - 1, last=True)


STAGES = ["ffn00", "ssm", "ffn01", "ffn10", "mla", "ffn11", "mixer", "moe"]


def build(nc, ins, out, per_turn, stages=STAGES):
    pr = Program(nc, ins, out, per_turn)
    pr.setup()
    pr.small_setup()
    for n in stages:
        if n == "ffn00":
            pr.ffn(0, 0)
        elif n == "ssm":
            ssm(pr)
        elif n == "ffn01":
            pr.ffn(0, 1)
        elif n == "ffn10":
            pr.mod_begin()
            pr.ffn(1, 0, ((0, 1), (2, 3)))
        elif n == "mla":
            mla(pr)
        elif n == "ffn11":
            pr.ffn(1, 1, ((4, 5), (6, 7)))
            pr.mod_end()
        elif n == "mixer":
            mixer(pr)
        elif n == "moe":
            moe(pr)
    finish(pr)
    return pr.sig.counted


INPUTS = ["x", "positions", "norm_w", "ffn_w_gate", "ffn_w_up", "ffn_w_down", "ssm_w_in", "ssm_conv_w", "ssm_conv_b",
          "ssm_dt_bias", "ssm_a_log", "ssm_d", "ssm_norm_w", "ssm_w_out", "mla_w_in", "mla_q_a_norm", "mla_kv_a_norm",
          "mla_w_q_b", "mla_w_kv_b", "mla_q_norm", "mla_k_norm", "mla_w_out", "c_2", "w_mod_2", "b_mod_2", "norm_mix_2",
          "norm_ffn_2", "w_in_2", "w_out_2", "out_gain_2", "sinks_2", "conv_w_2", "conv_b_2", "lru_wa_2", "lru_ba_2",
          "lru_wx_2", "lru_bx_2", "lru_lam_2", "fox_bf_2", "w_router_group_2", "b_router_group_2", "w_router_expert_2",
          "b_router_expert_2", "w_gate_2", "w_up_2", "w_down_2", "norm_final_2"]


def kernel(**inputs):
    import numpy as np
    import concourse.bacc as bacc
    from concourse.bass_utils import run_bass_kernel_spmd

    arrays = {name: np.ascontiguousarray(inputs[name]) for name in INPUTS}
    per_turn = {}
    for _ in range(3):
        nc = bacc.Bacc("TRN2", target_bir_lowering=False, num_devices=1)
        ins = {name: nc.dram_tensor(f"in_{name}", a.shape, mybir.dt.from_np(a.dtype), kind="ExternalInput").ap()
               for name, a in arrays.items()}
        out = nc.dram_tensor("out", (1, T, D), F32, kind="ExternalOutput").ap()
        per_turn = build(nc, ins, out, per_turn)
    r = run_bass_kernel_spmd(nc, [{f"in_{name}": a for name, a in arrays.items()}], core_ids=[0])
    return r.results[0]["out"]
```
